# Optimizing a Trainium2 kernel written in Bass

```python
import jax, jax.numpy as jnp
from jax import lax
import numpy as np

D_MODEL = 1024
BATCH = 1
SEQ = 1024
DEPTH = 1

ATTN_HEADS = 8
ATTN_KV_HEADS = 2
ATTN_HEAD_DIM = 64
WINDOW = 128
ATTN_BLOCK = 128
NUM_BUCKETS = 32
MAX_DISTANCE = 128
GLA_HEADS = 4
GLA_DK = 64
GLA_DV = 128
GLA_GATE_RANK = 16
GLA_GATE_NORM = 16.0
GLA_CHUNK = 64
D_FF = 4 * D_MODEL
EPS = 1e-6
N_MOD = 6

ATTN_Q = ATTN_HEADS * ATTN_HEAD_DIM
ATTN_KV = ATTN_KV_HEADS * ATTN_HEAD_DIM
GLA_K = GLA_HEADS * GLA_DK
GLA_V = GLA_HEADS * GLA_DV
SPLIT_SIZES = (ATTN_Q, ATTN_KV, ATTN_KV, GLA_K, GLA_K, GLA_V, GLA_V, GLA_GATE_RANK)
SPLIT_POINTS = tuple(int(s) for s in np.cumsum(SPLIT_SIZES)[:-1])
D_IN = int(sum(SPLIT_SIZES))
D_MIX = ATTN_Q + GLA_V

kernel_name = "hybrid_swa_gla_adaln_layer"

def rms_norm(x):
    x32 = x.astype(jnp.float32)
    return (x32 * lax.rsqrt(jnp.mean(x32 * x32, axis=-1, keepdims=True) + EPS)).astype(x.dtype)

def t5_causal_bucket(dist):
    max_exact = NUM_BUCKETS // 2
    d = np.maximum(dist, 0)
    large = max_exact + (np.log(np.maximum(d, max_exact) / max_exact)
                         / np.log(MAX_DISTANCE / max_exact) * (NUM_BUCKETS - max_exact)).astype(np.int32)
    large = np.minimum(large, NUM_BUCKETS - 1)
    return np.where(d < max_exact, d, large).astype(np.int32)

def sliding_window_attention(q, k, v, sinks, rel_bias):
    B, T, Hq, dh = q.shape
    Hkv = k.shape[2]
    G = Hq // Hkv
    L = ATTN_BLOCK
    nb = T // L
    qb = q.astype(jnp.float32).reshape(B, nb, L, Hkv, G, dh)
    kb = k.astype(jnp.float32).reshape(B, nb, L, Hkv, dh)
    vb = v.astype(jnp.float32).reshape(B, nb, L, Hkv, dh)
    pad = jnp.zeros_like(kb[:, :1])
    k2 = jnp.concatenate([jnp.concatenate([pad, kb[:, :-1]], axis=1), kb], axis=2)
    v2 = jnp.concatenate([jnp.concatenate([pad, vb[:, :-1]], axis=1), vb], axis=2)
    i = np.arange(L)[:, None]
    j = np.arange(2 * L)[None, :]
    dist = i + L - j
    band = (dist >= 0) & (dist < WINDOW)
    valid = np.broadcast_to(band, (nb, L, 2 * L)).copy()
    valid[0] &= np.broadcast_to(j >= L, (L, 2 * L))
    bucket = t5_causal_bucket(dist)
    bias = rel_bias.astype(jnp.float32)[bucket]
    bias = jnp.transpose(bias, (2, 0, 1)).reshape(Hkv, G, 1, L, 2 * L)
    s = jnp.einsum('bnqhgd,bnkhd->bhgnqk', qb, k2) * (dh ** -0.5) + bias
    s = jnp.where(valid, s, -jnp.inf)
    sink = sinks.astype(jnp.float32).reshape(Hkv, G)[None, :, :, None, None, None]
    m = jnp.maximum(jnp.max(s, axis=-1, keepdims=True), sink)
    p = jnp.exp(s - m)
    p = p / (jnp.sum(p, axis=-1, keepdims=True) + jnp.exp(sink - m))
    o = jnp.einsum('bhgnqk,bnkhd->bnqhgd', p, v2)
    return o.reshape(B, T, Hq * dh)

def gla_chunked(q, k, v, log_a):
    B, T, H, dk = q.shape
    dv = v.shape[-1]
    C = GLA_CHUNK
    n = T // C
    q = q.astype(jnp.float32).reshape(B, n, C, H, dk) * (dk ** -0.5)
    k = k.astype(jnp.float32).reshape(B, n, C, H, dk)
    v = v.astype(jnp.float32).reshape(B, n, C, H, dv)
    b = jnp.cumsum(log_a.astype(jnp.float32).reshape(B, n, C, H, dk), axis=2)
    b_last = b[:, :, -1:]
    q_t = q * jnp.exp(b)
    k_t = k * jnp.exp(-b)
    k_s = k * jnp.exp(b_last - b)
    causal = np.tril(np.ones((C, C), dtype=bool))
    A = jnp.where(causal, jnp.einsum('bnihd,bnjhd->bnhij', q_t, k_t), 0.0)
    o_intra = jnp.einsum('bnhij,bnjhv->bnihv', A, v)
    dS = jnp.einsum('bnjhd,bnjhv->bnhdv', k_s, v)
    decay = jnp.exp(b_last[:, :, 0])

    def step(S, inp):
        dS_n, dec_n = inp
        return dec_n[..., None] * S + dS_n, S

    S0 = jnp.zeros((B, H, dk, dv), jnp.float32)
    _, S_prev = lax.scan(step, S0, (jnp.moveaxis(dS, 1, 0), jnp.moveaxis(decay, 1, 0)))
    S_prev = jnp.moveaxis(S_prev, 0, 1)
    o_inter = jnp.einsum('bnihd,bnhdv->bnihv', q_t, S_prev)
    return (o_intra + o_inter).reshape(B, T, H, dv)

def setup_inputs(seed: int = 0) -> dict:
    key = jax.random.key(seed)
    ks = jax.random.split(key, 14)
    nrm = jax.random.normal
    f32 = jnp.float32
    return {
        "x": nrm(ks[0], (BATCH, SEQ, D_MODEL), f32),
        "c": nrm(ks[1], (BATCH, D_MODEL), f32),
        "w_ada": nrm(ks[2], (DEPTH, D_MODEL, N_MOD * D_MODEL), f32) * (0.5 * D_MODEL ** -0.5),
        "b_ada": nrm(ks[3], (DEPTH, N_MOD * D_MODEL), f32) * 0.01,
        "w_in": nrm(ks[4], (DEPTH, D_MODEL, D_IN), f32) * D_MODEL ** -0.5,
        "w_gate_up": nrm(ks[5], (DEPTH, GLA_GATE_RANK, GLA_K), f32) * GLA_GATE_RANK ** -0.5,
        "b_gate": nrm(ks[6], (DEPTH, GLA_K), f32) * 0.1,
        "gla_norm_g": 1.0 + 0.01 * nrm(ks[7], (DEPTH, GLA_DV), f32),
        "attn_sinks": nrm(ks[8], (DEPTH, ATTN_HEADS), f32) * 0.5,
        "rel_bias": nrm(ks[9], (NUM_BUCKETS, ATTN_HEADS), f32) * 0.5,
        "w_out": nrm(ks[10], (DEPTH, D_MIX, D_MODEL), f32) * D_MIX ** -0.5,
        "w_mlp_in": nrm(ks[11], (DEPTH, D_MODEL, D_FF), f32) * D_MODEL ** -0.5,
        "w_mlp_out": nrm(ks[12], (DEPTH, D_FF, D_MODEL), f32) * D_FF ** -0.5,
        "final_norm_g": 1.0 + 0.01 * nrm(ks[13], (D_MODEL,), f32),
    }

def reference(x, c, w_ada, b_ada, w_in, w_gate_up, b_gate, gla_norm_g, attn_sinks, rel_bias,
              w_out, w_mlp_in, w_mlp_out, final_norm_g):
    B, T, D = x.shape
    cond = jax.nn.silu(c)
    for l in range(DEPTH):
        ada = cond @ w_ada[l] + b_ada[l]
        shift1, scale1, gate1, shift2, scale2, gate2 = jnp.split(ada[:, None, :], N_MOD, axis=-1)

        h = rms_norm(x) * (1.0 + scale1) + shift1
        proj = h @ w_in[l]
        q_a, k_a, v_a, q_g, k_g, v_g, g_out, z_lr = jnp.split(proj, SPLIT_POINTS, axis=-1)

        attn = sliding_window_attention(
            q_a.reshape(B, T, ATTN_HEADS, ATTN_HEAD_DIM),
            k_a.reshape(B, T, ATTN_KV_HEADS, ATTN_HEAD_DIM),
            v_a.reshape(B, T, ATTN_KV_HEADS, ATTN_HEAD_DIM),
            attn_sinks[l], rel_bias).astype(x.dtype)

        log_a = jax.nn.log_sigmoid((z_lr @ w_gate_up[l] + b_gate[l]).astype(jnp.float32)) / GLA_GATE_NORM
        o = gla_chunked(
            q_g.reshape(B, T, GLA_HEADS, GLA_DK),
            k_g.reshape(B, T, GLA_HEADS, GLA_DK),
            v_g.reshape(B, T, GLA_HEADS, GLA_DV),
            log_a.reshape(B, T, GLA_HEADS, GLA_DK))
        o = rms_norm(o) * gla_norm_g[l].astype(jnp.float32)
        gla = (o.reshape(B, T, GLA_V) * jax.nn.silu(g_out.astype(jnp.float32))).astype(x.dtype)

        mix = jnp.concatenate([attn, gla], axis=-1) @ w_out[l]
        x = x + gate1 * mix

        h = rms_norm(x) * (1.0 + scale2) + shift2
        x = x + gate2 * (jnp.square(jax.nn.relu(h @ w_mlp_in[l])) @ w_mlp_out[l])
    return rms_norm(x) * final_norm_g


_drawn_inputs = setup_inputs


def setup_inputs(seed=0):
    import zlib

    import numpy as np

    out = dict(_drawn_inputs(seed))
    spreads = {}
    factors = {'b_ada': 3.586,
     'b_gate': 7.848,
     'gla_norm_g': 8.0,
     'attn_sinks': 8.0,
     'rel_bias': 3.143,
     'final_norm_g': 5.525}
    for name, (base, spread) in spreads.items():
        noise = np.random.default_rng([zlib.crc32(name.encode()), seed]).standard_normal(out[name].shape)
        drawn = base * np.exp(spread * noise) if base else spread * noise
        out[name] = __import__('jax').numpy.asarray(drawn.astype(out[name].dtype))
    for name, factor in factors.items():
        out[name] = (out[name] * factor).astype(out[name].dtype)
    return out
```

```python
import numpy as np
import concourse.bass as bass
from concourse import mybir
from concourse.alu_op_type import AluOpType as ALU

F32 = mybir.dt.float32
F32R = mybir.dt.float32r
I32 = mybir.dt.int32
ACT = mybir.ActivationFunctionType
AX = mybir.AxisListType
ds = bass.ds

P = 128
D = 1024
T = 1024
KT = D // P
NT = T // P
HALF = 512
HEADS = 8
DH = 64
BUCKETS = 32
MAX_DISTANCE = 128
GLA_HEADS = 4
DK = 64
DV = 128
CHUNK = 64
RANK = 16
GATE_NORM = 16.0
EPS = 1e-6
FF = 4096
GROUP = 512
NG = FF // GROUP
NCH = T // CHUNK
Q0, K0, V0, QG0, KG0, VG0, GO0, Z0 = 0, 512, 640, 768, 1024, 1280, 1792, 2304
SLOT = 2048
LOWEST = -3.0e38
KIB = 1024
DGE_SCRATCH = 2048

SLOT_F, SLOT_T, SLOT_O, SLOT_M = 0, 5, 9, 13
G_N1 = 0
G_F = G_N1 + 16
G_N1_HALVES = (G_N1, G_N1 + 10)
G_F_FIRST = (G_N1 + 8, G_N1 + 18)
G_Z = G_F + 20
G_V = G_Z + 2
G_G = G_V + 2
G_T = G_G + 4
G_O = G_T + 32
G_N2 = G_O + 32
G_M = G_N2 + 16
G_N2_HALVES = (G_N2, G_N2 + 10)
G_M_FIRST = (G_N2 + 8, G_N2 + 18)
SLOT_LAST = SLOT_M + 4 * NG - 1


def bucket_of(dist):
    max_exact = BUCKETS // 2
    d = np.maximum(dist, 0)
    large = max_exact + (np.log(np.maximum(d, max_exact) / max_exact)
                         / np.log(MAX_DISTANCE / max_exact) * (BUCKETS - max_exact)).astype(np.int32)
    return np.where(d < max_exact, d, np.minimum(large, BUCKETS - 1)).astype(np.int32)


def constants():
    onehot = np.zeros((BUCKETS + 1, 384), np.float32)
    dist = 255 - np.arange(384)
    valid = (dist >= 0) & (dist < P)
    onehot[np.where(valid, bucket_of(dist), BUCKETS), np.arange(384)] = 1.0
    j, i = np.arange(P)[:, None], np.arange(P)[None, :]
    tri = ((j <= i) & (j // CHUNK == i // CHUNK)).astype(np.float32)
    return {"identity": np.eye(P, dtype=np.float32), "reversal": np.eye(P, dtype=np.float32)[::-1].copy(), "bucket_onehot": onehot, "chunk_causal": tri}


class Chain:

    def __init__(self, eng, sem):
        self.eng, self.sem, self.count, self.turn, self.per_turn = eng, sem, 0, None, 0

    def link(self, instruction):
        instruction.then_inc(self.sem, 1)
        self.count += 1
        if self.turn is None:
            self.eng.wait_ge(self.sem, self.count)
        else:
            self.eng.wait_ge(self.sem, self.turn * self.per_turn + self.count)

    def enter(self, turn, per_turn):
        self.turn, self.per_turn, self.start = turn, per_turn, self.count

    def leave(self, turns):
        assert self.count - self.start == self.per_turn, (self.count, self.start, self.per_turn)
        self.count = self.start + turns * self.per_turn
        self.turn = None


def build(nc, x, c, w_ada, b_ada, w_in, w_gate_up, b_gate, gla_norm_g, attn_sinks, rel_bias,
          w_out, w_mlp_in, w_mlp_out, final_norm_g, identity, reversal, bucket_onehot, chunk_causal, out):
    x_d = x[0].rearrange("(t p) d -> p t d", p=P)
    out_d = out[0].rearrange("(t p) d -> p t d", p=P)
    w_ada_d = w_ada[0].rearrange("(p k) n -> p k n", k=KT)
    w_in_d = w_in[0].rearrange("(k p) n -> p k n", p=P)
    w_out_d = w_out[0]
    w_up_d = w_mlp_in[0].rearrange("(k p) n -> p k n", p=P)
    w_down_d = w_mlp_out[0]
    bias_rows = nc.dram_tensor("bias_rows", [HEADS, 384], F32, kind="Internal")

    base = DGE_SCRATCH + 128

    def at(kib, name, shape, dt=F32):
        return nc.alloc_sbuf_tensor_at(name, [P, *shape], dt, offset=base + int(kib * KIB))

    act_hi = at(0, "act_hi", [KT, T], F32R)
    act_lo = at(32, "act_lo", [KT, T], F32R)
    ada_w_first = at(0, "ada_w_first", [2 * KT, D])
    x_in = at(64, "x_in", [NT, D])
    x_nrm = at(96, "x_nrm", [NT, D])
    q_t = at(64, "q_t", [4, T])
    k_t = at(80, "k_t", [P + T])
    v_tok = at(84.5, "v_tok", [NT + 1, P])
    gq_t = at(89, "gq_t", [2, T])
    gk_t = at(97, "gk_t", [2, T])
    gks_t = at(105, "gks_t", [2, T])
    gv_tok = at(113, "gv_tok", [NT, GLA_HEADS * DV])
    bias_rev = at(113, "bias_rev", [HEADS, 2 * P])
    hid_hi = at(64, "hid_hi", [2, GROUP // P, T], F32R)
    hid_lo = at(96, "hid_lo", [2, GROUP // P, T], F32R)
    x1_nrm = at(64, "x1_nrm", [NT, D])
    x1 = at(130, "x1", [NT, D])
    ada_w = at(130, "ada_w", [4, D])
    silu_g = at(130, "silu_g", [NT, GLA_HEADS * DV])
    z_t = at(130, "z_t", [T])
    w_gate = at(134, "w_gate", [GLA_HEADS * DK])
    ada_acc = at(146, "ada_acc", [2, D])
    cum = at(146, "cum", [2, T])
    bias = at(146, "bias", [HEADS, 2 * P])
    ada_b = at(154, "ada_b", [D])
    z_raw = at(158, "z_raw", [KT, RANK])
    z_hi = at(158.5, "z_hi", [KT, RANK], F32R)
    z_lo = at(159, "z_lo", [KT, RANK], F32R)
    tmp_a = at(154, "tmp_a", [T])
    tmp_b = at(158, "tmp_b", [T])
    a_mask = at(154, "a_mask", [GLA_HEADS, P])
    state_a = at(156, "state_a", [2, DV])
    state_b = at(157, "state_b", [2, DV])
    gla_out = at(158, "gla_out", [GLA_HEADS, DV])
    gks_tok = at(160, "gks_tok", [2 * P])
    raw = at(162, "raw", [2, SLOT])
    prob = at(162, "prob", [HEADS, 2 * P])
    prob_t = at(170, "prob_t", [2, 2, 4 * P])
    w_hi = at(178, "w_hi", [2, SLOT], F32R)
    w_lo = at(194, "w_lo", [2, SLOT], F32R)
    gate1 = at(210, "gate1", [D])
    gate2 = at(214, "gate2", [D])
    ident = at(218, "ident", [P])
    ones = at(218.5, "ones", [P])
    tri = at(219, "tri", [P])
    small = at(220, "small", [400])
    rev = at(219.5, "rev", [P])
    taken = [0]

    def vec(n):
        taken[0] += n
        return small[:, taken[0] - n:taken[0]]

    c_in, c_exp, cond = vec(KT), vec(KT), vec(KT)
    ada_col = vec(6 * KT)
    b_gate_c = vec(2)
    b_col = vec(6 * KT)
    n_sink = vec(HEADS)
    rel_ext = vec(HEADS)
    decay, cum_last = vec(2 * NCH), vec(2 * NCH)
    ssq, var, lnv, rstd, newt = vec(NT), vec(NT), vec(NT), vec(NT), vec(NT)
    mx, nm, sd, es, rs, den = (vec(HEADS) for _ in range(6))
    gss, gvar, gln, grs, gnt = (vec(GLA_HEADS) for _ in range(5))
    decay3 = decay.rearrange("p (t c) -> p t c", t=2)
    cum_last3 = cum_last.rearrange("p (t c) -> p t c", t=2)

    bank = [nc.alloc_psum_tensor(f"bank{i}", [P, 512], F32) for i in range(8)]

    def sem(name):
        return nc.alloc_semaphore(name)

    s_c, s_const, s_small = sem("c_landed"), sem("const_landed"), sem("small_landed")
    s_x = [sem(f"x_landed{i}") for i in range(NT)]
    s_ada_first = [sem(f"ada_first_landed{i}") for i in range(KT)]
    s_ident = sem("identity_landed")
    s_b_rows, s_b_full, s_b_col = sem("b_rows_landed"), sem("b_col_full"), sem("b_col_ready")
    s_ada_w = [sem(f"ada_w_landed{i}") for i in range(4)]
    s_ada_b = sem("ada_b_landed")
    s_z_raw = sem("z_raw_landed")
    s_raw = [sem("raw_landed0"), sem("raw_landed1")]
    s_c_exp, s_ada_used, s_ada_sum, s_ada_full, s_gate_full, s_gate_copied, s_ada_col = (
        sem(n) for n in ("c_exp", "ada_used", "ada_summed", "ada_full", "gate_full", "gate_copied", "ada_col"))
    s_gated, s_hi, s_lo = (sem(n) for n in ("raw_gated", "slot_hi", "slot_lo"))
    s_full, s_free = sem("psum_full"), sem("psum_free")
    s_sq, s_var, s_root, s_nrm = (sem(n) for n in ("squares", "variance", "root", "normed"))
    s_set = sem("memsets")
    s_bias_full, s_bias_read = sem("bias_turned"), sem("bias_read")
    s_rows_full, s_rows, s_rows_out, s_bias = (
        sem(n) for n in ("bias_rows_full", "bias_rows_copied", "bias_rows_written", "bias_landed"))
    s_act = sem("act_stage")
    s_zhi, s_zlo = sem("z_hi_done"), sem("z_lo_done")
    s_gate_v, s_gate_s = sem("gates_by_vector"), sem("gates_by_scalar")
    s_sg_e = sem("silu_exp")
    s_sc_full, s_sc_free, s_nm, s_exp, s_pn = (
        sem(n) for n in ("scores_full", "scores_read", "neg_max", "exps", "probs_ready"))
    s_pt_full, s_pt_a, s_pt_v = sem("probs_t_full"), sem("probs_t_by_scalar"), sem("probs_t_by_vector")
    s_oa_full, s_oa_hi, s_oa_lo = sem("attn_out_full"), sem("attn_out_hi"), sem("attn_out_lo")
    s_at_full, s_at = sem("gla_a_full"), sem("gla_a_masked")
    s_ks_full, s_ks = sem("gla_ks_full"), sem("gla_ks_copied")
    s_ds_full, s_st_b, s_st_a = sem("gla_ds_full"), sem("state_b_ready"), sem("state_a_ready")
    s_go_full, s_gsq, s_gvar, s_grt, s_og = (
        sem(n) for n in ("gla_o_full", "gla_squares", "gla_variance", "gla_root", "gla_out_ready"))
    s_gt_full, s_gt_hi, s_gt_lo = sem("gla_out_t_full"), sem("gla_out_t_hi"), sem("gla_out_t_lo")
    s_x1 = [sem("x1_landed0"), sem("x1_landed1")]
    s_gfin = sem("final_gain_landed")
    s_d1, s_fin, s_out = sem("down_added"), sem("final_ready"), sem("out_written")
    s_vch, s_sch = sem("vector_own"), sem("scalar_own")
    s_gn, s_wg = sem("gla_gain_landed"), sem("w_gate_landed")

    gate_rows = {2: gate1, 5: gate2}
    b_rows = gate1[0:6 * KT, 0:P]
    onehot_sb = gate2[0:BUCKETS + 1, 0:384]
    rows_sb = gate2[0:HEADS, 512:512 + 384]
    gain_col = vec(1)

    LAND = 64

    block = nc.Block()
    with block:
        @block.sync
        def _(sp):
            sp.dma_start(c_in, c[0].rearrange("(p k) -> p k", k=KT)).then_inc(s_c, 16)

            def ada_first(part):
                for j in range(KT // 2):
                    sp.dma_start(ada_w_first[:, part * KT + 2 * j:part * KT + 2 * j + 2, :],
                                 w_ada_d[:, 2 * j:2 * j + 2, part * D:(part + 1) * D])\
                        .then_inc(s_ada_first[part * KT // 2 + j], 16)

            def fill(s, par, sources):
                if not isinstance(s, int) or s >= 2:
                    sp.wait_ge(s_lo, s - 1)
                for dst, src in sources(par):
                    sp.dma_start(dst, src).then_inc(s_raw[par], 16)

            def raw_k(par):
                return raw[:, par, :].rearrange("p (k c) -> p k c", k=KT)

            def q_columns(s):
                return lambda par: [(raw_k(par)[:, :, m * P + g * DH:m * P + g * DH + DH],
                                     w_in_d[:, :, Q0 + g * 256 + (2 * s + m) * DH:Q0 + g * 256 + (2 * s + m) * DH + DH])
                                    for m in range(2) for g in range(2)]

            ada_first(0)
            sp.dma_start(b_rows, b_ada[0].rearrange("(k p) -> k p", p=P)).then_inc(s_b_rows, 16)
            sp.dma_start(ident[:, :], identity).then_inc(s_ident, 16)
            fill(0, 0, q_columns(0))
            ada_first(1)
            for t in range(NT):
                sp.dma_start(x_in[:, t, :], x_d[:, t, :]).then_inc(s_x[t], 16)
            fill(1, 1, q_columns(1))
            sp.dma_start(tri[:, :], chunk_causal).then_inc(s_const, 16)
            sp.dma_start(rev[:, :], reversal).then_inc(s_const, 16)
            sp.dma_start(onehot_sb, bucket_onehot).then_inc(s_small, 16)
            sp.dma_start(rel_ext[0:BUCKETS, :], rel_bias).then_inc(s_small, 16)
            sp.dma_start(n_sink, attn_sinks[0:1, :].broadcast_to([P, HEADS])).then_inc(s_small, 16)
            with nc.allow_non_contiguous_dma(reason="256 gate biases, one a partition"):
                sp.dma_start(b_gate_c, b_gate[0].rearrange("(t p) -> p t", p=P)).then_inc(s_small, 16)
                sp.dma_start(z_raw[:, :, :], w_in_d[:, :, Z0:Z0 + RANK]).then_inc(s_z_raw, 16)

            def columns(w, c0, width=256):
                return lambda par: [(raw_k(par)[:, 2 * j:2 * j + 2, :], w[:, 2 * j:2 * j + 2, ds(c0, width)])
                                    for j in range(4)]

            def out_rows(c0):
                def parts(par):
                    r = raw_k(par)
                    yield r[0:DH, 0:4, :], w_out_d[0:256, c0:c0 + 256].rearrange("(t p) n -> p t n", p=DH)
                    yield r[DH:P, 0:4, :], w_out_d[256:512, c0:c0 + 256].rearrange("(t p) n -> p t n", p=DH)
                    for j in range(2):
                        yield (r[:, 4 + 2 * j:6 + 2 * j, :],
                               w_out_d[512 + 256 * j:768 + 256 * j, c0:c0 + 256].rearrange("(t p) n -> p t n", p=P))
                return parts

            def down_rows(g, half):
                def parts(par):
                    for j in range(4):
                        yield (raw[:, par, j * 512:(j + 1) * 512],
                               w_down_d[ds(g * GROUP + j * P, P), half * 512:half * 512 + 512])
                return parts

            for s, c0 in ((2, K0), (3, QG0), (4, KG0)):
                fill(s, s % 2, columns(w_in_d, c0))
            sp.wait_ge(s_rows_out, 16)
            sp.wait_ge(s_free, G_F_FIRST[1])
            shifted = bass.AP(tensor=bias_rows, offset=0, ap=[[1, P], [384, HEADS], [1, 2 * P]])
            sp.dma_start(bias_rev[:, :, :], shifted).then_inc(s_bias, 16)
            for s in range(4):
                fill(SLOT_T + s, (SLOT_T + s) % 2, columns(w_in_d, VG0 + 256 * s))
            for s in range(2):
                fill(SLOT_O + s, (SLOT_O + s) % 2, out_rows(256 * s))
            sp.wait_ge(s_oa_lo, NT)
            sp.wait_ge(s_gt_lo, NT)
            for h in range(2):
                for t in range(4 * h, 4 * h + 4):
                    sp.dma_start(x1[:, t, :], x_d[:, t, :]).then_inc(s_x1[h], 16)
                fill(SLOT_O + 2 + h, (SLOT_O + h) % 2, out_rows(256 * (2 + h)))
            for half in range(2):
                fill(SLOT_M + half, (SLOT_M + half) % 2, columns(w_up_d, 256 * half))

            def pair(g):
                for half in range(2):
                    fill(SLOT_M + 2 + 4 * g + half, (SLOT_M + half) % 2,
                         columns(w_up_d, (g + 1) * GROUP + 256 * half))
                for half in range(2):
                    fill(SLOT_M + 4 + 4 * g + half, (SLOT_M + half) % 2, down_rows(g, half))

            with sp.Fori(0, NG - 1, 1) as g:
                pair(g)
            for half in range(2):
                fill(SLOT_LAST - 1 + half, (SLOT_M + half) % 2, down_rows(NG - 1, half))
            sp.wait_ge(s_lo, SLOT_O + 4)
            sp.dma_start(gate1[:, :], final_norm_g.rearrange("(a d) -> a d", a=1).broadcast_to([P, D]))\
                .then_inc(s_gfin, 16)
            for t in range(NT):
                sp.wait_ge(s_fin, t + 1)
                sp.dma_start(out_d[:, t, :], x1[:, t, :]).then_inc(s_out, 16)
            sp.wait_ge(s_out, 16 * NT)

        @block.gpsimd
        def _(pool):
            pool.memset(ones[:, :], 1.0).then_inc(s_set, 1)
            pool.wait_ge(s_set, 1)
            pool.memset(rel_ext[BUCKETS:BUCKETS + 1, :], LOWEST).then_inc(s_set, 1)
            for part in range(2, 6):
                if part in gate_rows:
                    if part == 5:
                        pool.wait_ge(s_ada_sum, 1)
                    pool.dma_start(ada_b[0:1, :], b_ada[0:1, part * D:(part + 1) * D]).then_inc(s_ada_b, 16)
                if part == 2:
                    pool.wait_ge(s_x[NT - 1], 16)
                for k in range(KT):
                    j = (part - 2) * KT + k
                    if j >= 4:
                        pool.wait_ge(s_ada_used, 2 * KT + j - 3)
                    pool.dma_start(ada_w[:, j % 4, :], w_ada_d[:, k, part * D:(part + 1) * D])\
                        .then_inc(s_ada_w[j % 4], 16)
                if part == 2:
                    pool.wait_ge(s_rows, 1)
                    pool.dma_start(bias_rows.ap(), rows_sb).then_inc(s_rows_out, 16)
            pool.wait_ge(s_ada_used, 6 * KT)
            pool.dma_start(w_gate[0:RANK, :], w_gate_up[0]).then_inc(s_wg, 16)
            with nc.allow_non_contiguous_dma(reason="128 gains, one a partition"):
                pool.dma_start(gain_col, gla_norm_g[0].rearrange("(p a) -> p a", a=1)).then_inc(s_gn, 16)

        @block.tensor
        def _(pe):
            def act(part):
                return act_lo if part else act_hi

            def wsl(part, par):
                return (w_lo if part else w_hi)[:, par, :]

            def stationary_half(par, half, g, turned=None):
                for m in range(2):
                    if not isinstance(g, int) or g + m >= 4:
                        pe.wait_ge(s_free, g + m - 3)
                    n = 0
                    for k in range(KT):
                        if turned is not None and m == 0:
                            pe.wait_ge(s_free, turned + k)
                        for a, b in ((0, 0), (0, 1), (1, 0)):
                            w = wsl(a, par)[:, k * 256 + m * P:k * 256 + m * P + P]
                            mm = pe.matmul(bank[2 * half + m][:, :], w,
                                           act(b)[:, k, half * HALF:half * HALF + HALF],
                                           start=(n == 0), stop=(n == 3 * KT - 1))
                            n += 1
                    mm.then_inc(s_full, 1)

            def stationary_weights(s, par, g):
                pe.wait_ge(s_lo, s + 1)
                for half in range(2):
                    stationary_half(par, half, g + 2 * half)

            def moving_weights(s, par, g, tiles, stat, kt, width, split_last=False):
                pe.wait_ge(s_lo, s + 1)
                for i, t in enumerate(tiles):
                    if split_last and t == 2:
                        pe.wait_ge(s_oa_lo, NT)
                    if split_last and t == NT - 1:
                        pe.wait_ge(s_gt_lo, NT)
                    if not isinstance(g, int) or g + i >= 4:
                        pe.wait_ge(s_free, g + i - 3)
                    n = 0
                    for k in range(kt):
                        for a, b in ((0, 0), (0, 1), (1, 0)):
                            mm = pe.matmul(bank[i % 4][:, 0:width], stat(a, k, t),
                                           wsl(b, par)[:, k * width:(k + 1) * width],
                                           start=(n == 0), stop=(n == 3 * kt - 1))
                            n += 1
                    mm.then_inc(s_full, 1)

            def tok_act(a, k, t):
                return act(a)[:, k, t * P:(t + 1) * P]

            def ada(part):
                acc = ada_acc[:, part % 2, :]
                if part in gate_rows:
                    pe.wait_ge(s_ada_sum, 1 if part == 2 else 2)
                    if part == 2:
                        pe.wait_ge(s_b_col, 1)
                    if part == 5:
                        pe.wait_ge(s_gate_copied, 1)
                    for h in range(2):
                        mm = pe.matmul(bank[5 + h][:, :], ones[:, :], acc[:, h * 512:(h + 1) * 512], start=True, stop=True)
                    mm.then_inc(s_gate_full, 1)
                else:
                    pe.wait_ge(s_ada_used, (part + 1) * KT)
                    if part == 3:
                        pe.wait_ge(s_ada_col, 2)
                    for k in range(KT):
                        mm = pe.matmul(bank[4][:, part * KT + k:part * KT + k + 1], acc[:, k * P:(k + 1) * P],
                                       ones[:, 0:1], start=True, stop=True)
                    mm.then_inc(s_ada_full, 1)

            def turn_half(src, half, g, nrm):
                pe.wait_ge(s_nrm, nrm)
                for k in range(KT):
                    if g + k >= 4:
                        pe.wait_ge(s_free, g + k - 3)
                    for t in range(4):
                        mm = pe.transpose(bank[(g + k) % 4][:, t * P:(t + 1) * P],
                                          src[:, 4 * half + t, k * P:(k + 1) * P], ident[:, :])
                    mm.then_inc(s_full, 1)

            def turn_and_first_slot(src, norms, halves, first, s, par):
                for half in range(2):
                    turn_half(src, half, halves[half], norms + half + 1)
                    if half == 0:
                        pe.wait_ge(s_lo, s + 1)
                    stationary_half(par, half, first[half], halves[half] + 1)

            pe.wait_ge(s_b_rows, 16)
            pe.wait_ge(s_ident, 16)
            pe.transpose(bank[5][:, 0:6 * KT], b_rows, ident[0:6 * KT, 0:6 * KT]).then_inc(s_b_full, 1)
            pe.wait_ge(s_set, 2)
            ada(0)
            ada(1)
            pe.wait_ge(s_small, 64)
            pe.matmul(bank[7][0:HEADS, 0:384], rel_ext[0:BUCKETS + 1, :], onehot_sb, start=True, stop=True)\
                .then_inc(s_rows_full, 1)
            turn_and_first_slot(x_nrm, 0, G_N1_HALVES, G_F_FIRST, 0, 0)
            for s in range(1, 5):
                stationary_weights(s, s % 2, G_F + 4 * s)
                ada(s + 1)
            pe.wait_ge(s_zlo, 1)
            for half in range(2):
                pe.wait_ge(s_free, G_Z + half - 3)
                n = 0
                for k in range(KT):
                    for a, b in ((0, 0), (0, 1), (1, 0)):
                        mm = pe.matmul(bank[half][0:RANK, :], (z_lo if a else z_hi)[:, k, :],
                                       act(b)[:, k, half * HALF:half * HALF + HALF],
                                       start=(n == 0), stop=(n == 3 * KT - 1))
                        n += 1
                mm.then_inc(s_full, 1)
            for half in range(2):
                pe.wait_ge(s_free, G_V + half - 3)
                for t in range(4):
                    mm = pe.transpose(bank[2 + half][:, t * P:(t + 1) * P],
                                      gks_t[:, 0, (4 * half + t) * P:(4 * half + t + 1) * P], ident[:, :])
                mm.then_inc(s_full, 1)
            pe.wait_ge(s_free, G_Z + 2)
            pe.wait_ge(s_wg, 16)
            for tt in range(2):
                for half in range(2):
                    i = 2 * tt + half
                    pe.wait_ge(s_free, G_G + i - 3)
                    pe.matmul(bank[i][:, :], w_gate[0:RANK, tt * P:(tt + 1) * P],
                              z_t[0:RANK, half * HALF:(half + 1) * HALF], start=True, stop=True).then_inc(s_full, 1)
            pe.wait_ge(s_bias, 16)
            pe.wait_ge(s_const, 32)
            pe.wait_ge(s_gate_copied, 2)
            pe.wait_ge(s_ada_col, 4)
            pe.wait_ge(s_rows, 1)
            for i in range(4):
                mm = pe.matmul(bank[4 + i][:, :], rev[:, :], bias_rev[:, 2 * i:2 * i + 2, :], start=True, stop=True)
            mm.then_inc(s_bias_full, 1)
            with pe.Fori(0, 4, 2) as s:
                for j in range(2):
                    moving_weights(SLOT_T + s + j, (SLOT_T + j) % 2, G_T + 8 * (s + j), range(NT), tok_act, KT, 256)

            def tok(n):
                return slice(n * P, (n + 1) * P)

            def probs_turned(n, g):
                pe.wait_ge(s_pn, 2 * n + g + 1)
                for kb in range(2):
                    if g == 1:
                        pe.wait_ge((s_pt_a, s_pt_v)[kb], 2 * n + 1)
                    elif n > 0 and kb == 0:
                        pe.wait_ge(s_oa_lo, n)
                    elif n > 0:
                        pe.wait_ge(s_pt_v, 2 * n)
                    for h in range(4):
                        mm = pe.transpose(bank[2 + kb][:, h * P:(h + 1) * P],
                                          prob[:, 4 * g + h, kb * P:(kb + 1) * P], ident[:, :])
                    mm.then_inc(s_pt_full, 1)

            def attend(n):
                for g in range(2):
                    pe.wait_ge(s_pt_a, 2 * n + g + 1)
                    pe.wait_ge(s_pt_v, 2 * n + g + 1)
                for g in range(2):
                    for kb in range(2):
                        mm = pe.matmul(bank[2][g * DH:(g + 1) * DH, :], v_tok[:, n + kb, g * DH:(g + 1) * DH],
                                       prob_t[:, g, kb, :], start=(kb == 0), stop=(kb == 1))
                mm.then_inc(s_oa_full, 1)

            def out_turned(n):
                pe.wait_ge(s_og, n + 1)
                for h in range(GLA_HEADS):
                    mm = pe.transpose(bank[4][:, h * P:(h + 1) * P], gla_out[:, h, :], ident[:, :])
                mm.then_inc(s_gt_full, 1)

            def front(n, g, first=False):
                for hp in (2 * g, 2 * g + 1):
                    if not first or hp >= 2:
                        pe.wait_ge(s_sc_free, 4 * n + hp - 1)
                    for j in range(2):
                        h = 2 * hp + j
                        t = h % 4
                        q = q_t[g * DH:(g + 1) * DH, t, tok(n)]
                        if first:
                            mm = pe.matmul(bank[hp % 2][:, j * 256 + P:j * 256 + 256], q,
                                           k_t[g * DH:(g + 1) * DH, P:2 * P], start=True, stop=True)
                        else:
                            mm = pe.matmul(bank[hp % 2][:, j * 256:j * 256 + 256], q,
                                           k_t[g * DH:(g + 1) * DH, n * P:(n + 2) * P], start=True, stop=True)
                    mm.then_inc(s_sc_full, 1)

            def gla_scores(n, first=False):
                if not first:
                    pe.wait_ge(s_st_a, n + 1)
                for h in range(GLA_HEADS):
                    r = slice((h % 2) * DK, (h % 2) * DK + DK)
                    mm = pe.matmul(bank[(5, 7)[h % 2]][:, h // 2 * P:(h // 2 + 1) * P], gk_t[r, h // 2, tok(n)], gq_t[r, h // 2, tok(n)],
                                   start=True, stop=True)
                mm.then_inc(s_at_full, 1)
                if not first:
                    pe.wait_ge(s_og, n)
                for tt in range(2):
                    mm = pe.transpose(bank[6][:, tt * P:(tt + 1) * P], gks_t[:, tt, tok(n)], ident[:, :])
                mm.then_inc(s_ks_full, 1)

            def out_cols(h, rows):
                return bank[(6, 4)[h % 2]][rows, h // 2 * P:(h // 2 + 1) * P]

            def gla_out_of(n):
                pe.wait_ge(s_at, n + 1)
                pe.wait_ge(s_ks, n + 1)
                for ch in range(2):
                    for h in range(GLA_HEADS):
                        r = slice(ch * CHUNK, ch * CHUNK + CHUNK)
                        gv = gv_tok[r, n, h * DV:(h + 1) * DV]
                        c0 = h // 2 * P
                        mm = pe.matmul(bank[(5, 7)[ch]][(h % 2) * DK:(h % 2) * DK + DK, c0:c0 + P],
                                       gks_tok[r, h * DK:(h + 1) * DK], gv, start=True, stop=True)
                mm.then_inc(s_ds_full, 1)
                for h in (0, 2, 1, 3):
                    if h == 1 and n > 0:
                        pe.wait_ge(s_gt_lo, n)
                    gv = gv_tok[:, n, h * DV:(h + 1) * DV]
                    pe.matmul(out_cols(h, slice(0, P)), a_mask[:, h, :], gv, start=(h < 2), stop=False,
                              skip_group_check=True)
                for ch, ready, state in ((0, s_st_a, state_a), (1, s_st_b, state_b)):
                    pe.wait_ge(ready, n + 1)
                    for h in range(GLA_HEADS):
                        r = slice((h % 2) * DK, (h % 2) * DK + DK)
                        mm = pe.matmul(out_cols(h, slice(ch * CHUNK, (ch + 1) * CHUNK)),
                                       gq_t[r, h // 2, n * P + ch * CHUNK:n * P + (ch + 1) * CHUNK], state[r, h // 2, :],
                                       start=False, stop=True, skip_group_check=True)
                mm.then_inc(s_go_full, 1)

            pe.wait_ge(s_free, G_O)
            pe.wait_ge(s_gate_v, 10)
            front(0, 0, first=True)
            front(0, 1, first=True)
            pe.wait_ge(s_bias_read, 1)
            gla_scores(0, first=True)
            gla_out_of(0)
            for n in range(1, NT):
                for g in range(2):
                    probs_turned(n - 1, g)
                    front(n, g)
                attend(n - 1)
                out_turned(n - 1)
                gla_scores(n)
                gla_out_of(n)
            for g in range(2):
                probs_turned(NT - 1, g)
            attend(NT - 1)
            out_turned(NT - 1)

            pe.wait_ge(s_pt_v, 2 * NT)
            with pe.Fori(0, 4, 2) as s:
                for j in range(2):
                    moving_weights(SLOT_O + s + j, (SLOT_O + j) % 2, G_O + 8 * (s + j), range(NT), tok_act, KT, 256,
                                   split_last=True)
            turn_and_first_slot(x1_nrm, 2, G_N2_HALVES, G_M_FIRST, SLOT_M, SLOT_M % 2)
            stationary_weights(SLOT_M + 1, (SLOT_M + 1) % 2, G_M + 4)

            def hidden(buf):
                return lambda a, k, t: (hid_lo if a else hid_hi)[:, buf, k, t * P:(t + 1) * P]

            def up(g, s, base_group):
                for half in range(2):
                    stationary_weights(s + half, (SLOT_M + half) % 2, base_group + 4 * half)

            def down(g_buf, s, base_group):
                for half in range(2):
                    moving_weights(s + half, (SLOT_M + half) % 2, base_group + 8 * half, range(NT),
                                   hidden(g_buf), GROUP // P, 512)

            def pair(g, buf):
                up(g + 1, SLOT_M + 2 + 4 * g, G_M + 8 + 24 * g)
                down(buf, SLOT_M + 4 + 4 * g, G_M + 16 + 24 * g)

            with pe.Fori(0, NG - 2, 2) as g:
                pair(g, 0)
                pair(g + 1, 1)
            pair(NG - 2, 0)
            pe.wait_ge(s_free, G_M + 8 + 24 * (NG - 2) + 8)
            down(1, SLOT_LAST - 1, G_M + 8 + 24 * (NG - 1))

        @block.vector
        def _(v):
            own = Chain(v, s_vch)

            def gate_slot(s, par, row, kt, width):
                o = raw[:, par, :].rearrange("p (k c) -> p k c", k=kt)
                v.tensor_tensor(o, o, row.unsqueeze(1).broadcast_to([P, kt, width]), ALU.mult).then_inc(s_gated, 1)

            def gate_out_slot(s, par, row):
                o = raw[:, par, :].rearrange("p (k c) -> p k c", k=KT)
                rows = row.unsqueeze(1).broadcast_to([P, KT // 2, 256])
                v.tensor_tensor(o[:, 0:KT // 2], o[:, 0:KT // 2], rows, ALU.mult)
                v.scalar_tensor_tensor(o[:, KT // 2:KT], o[:, KT // 2:KT], gain_col, rows, ALU.mult, ALU.mult)\
                    .then_inc(s_gated, 1)

            def split_lo(s, par):
                v.wait_ge(s_hi, s + 1)
                v.tensor_tensor(w_lo[:, par, :], raw[:, par, :], w_hi[:, par, :], ALU.subtract).then_inc(s_lo, 1)

            def landed(par, count):
                v.wait_ge(s_raw[par], count)

            def full(g):
                v.wait_ge(s_full, g + 1)

            def newton(y, vv, t):
                own.link(v.tensor_tensor(t, y, y, ALU.mult))
                own.link(v.tensor_tensor(t, t, vv, ALU.mult))
                own.link(v.tensor_scalar(t, t, -0.5, 1.5, ALU.mult, ALU.add))
                own.link(v.tensor_tensor(y, y, t, ALU.mult))

            def ada_part(part):
                acc = ada_acc[:, part % 2, :]
                if part >= 2:
                    done = sum(1 for p in range(part - 1) if p not in gate_rows)
                    v.wait_ge(s_ada_full, done)
                    if part == 4:
                        v.wait_ge(s_gate_full, 1)
                for k in range(KT):
                    if part < 2:
                        v.wait_ge(s_ada_first[(part * KT + k) // 2], 16)
                        w = ada_w_first[:, part * KT + k, :]
                    else:
                        j = (part - 2) * KT + k
                        v.wait_ge(s_ada_w[j % 4], 16 * (j // 4 + 1))
                        w = ada_w[:, j % 4, :]
                    if k == 0:
                        ins = v.tensor_scalar(acc, w, cond[:, k:k + 1], None, ALU.mult)
                    else:
                        v.wait_ge(s_ada_used, part * KT + k)
                        ins = v.scalar_tensor_tensor(acc, w, cond[:, k:k + 1], acc, ALU.mult, ALU.add)
                    ins.then_inc(s_ada_used, 1)
                if part in gate_rows:
                    v.wait_ge(s_ada_used, (part + 1) * KT)
                    v.wait_ge(s_ada_b, 16 if part == 2 else 32)
                    v.tensor_tensor(acc[0:1, :], acc[0:1, :], ada_b[0:1, :], ALU.add).then_inc(s_ada_sum, 1)

            def ada_column(part, nth):
                v.wait_ge(s_ada_full, nth)
                v.scalar_tensor_tensor(ada_col[:, part * KT:(part + 1) * KT], bank[4][:, part * KT:(part + 1) * KT],
                                       1.0 if part in (1, 4) else 0.0, b_col[:, part * KT:(part + 1) * KT],
                                       ALU.add, ALU.add).then_inc(s_ada_col, 1)

            def norm_var(half, norms):
                cols = slice(4 * half, 4 * half + 4)
                v.wait_ge(s_sq, norms + half + 1)
                v.tensor_scalar(var[:, cols], ssq[:, cols], 1.0 / D, EPS, ALU.mult, ALU.add).then_inc(s_var, 1)

            def norm_scale(src, dst, half, norms):
                cols = slice(4 * half, 4 * half + 4)
                v.wait_ge(s_root, norms + half + 1)
                newton(rstd[:, cols], var[:, cols], newt[:, cols])
                for t in range(4 * half, 4 * half + 4):
                    ins = v.tensor_scalar(dst[:, t, :], src[:, t, :], rstd[:, t:t + 1], None, ALU.mult)
                ins.then_inc(s_nrm, 1)

            def norm_lo(half, k, g, stages):
                v.wait_ge(s_act, stages + k + 1)
                v.tensor_tensor(act_lo[:, k, half * HALF:(half + 1) * HALF], bank[(g + k) % 4][:, :],
                                act_hi[:, k, half * HALF:(half + 1) * HALF], ALU.subtract).then_inc(s_free, 1)

            v.wait_ge(s_c_exp, 1)
            own.link(v.tensor_scalar(c_exp, c_exp, 1.0, None, ALU.add))
            own.link(v.reciprocal(c_exp, c_exp))
            own.link(v.tensor_tensor(cond, c_in, c_exp, ALU.mult))
            ada_part(0)
            split_lo(0, 0)
            v.wait_ge(s_b_full, 1)
            v.tensor_copy(b_col, bank[5][:, 0:6 * KT]).then_inc(s_b_col, 1)
            ada_part(1)
            v.wait_ge(s_b_col, 1)
            norm_var(0, 0)
            norm_scale(x_in, x_nrm, 0, 0)
            ada_column(0, 2)
            ada_column(1, 2)
            dests = {0: [(q_t, 0), (q_t, 1)], 1: [(q_t, 2), (q_t, 3)], 3: [(gq_t, 0), (gq_t, 1)],
                     4: [(gk_t, 0), (gk_t, 1)]}

            def features(s, half, g):
                for m in range(2):
                    full(g + m)
                    if s == 2:
                        dst = (k_t[:, P + half * HALF:P + (half + 1) * HALF] if m == 0 else
                               gks_t[:, 0, half * HALF:(half + 1) * HALF])
                    else:
                        buf, tile = dests[s][m]
                        dst = buf[:, tile, half * HALF:(half + 1) * HALF]
                    v.tensor_copy(dst, bank[2 * half + m][:, :]).then_inc(s_free, 1)

            for k in range(KT):
                norm_lo(0, k, G_N1_HALVES[0], 0)
                if k == 2:
                    norm_var(1, 0)
            norm_scale(x_in, x_nrm, 1, 0)
            split_lo(1, 1)
            v.wait_ge(s_rows_full, 1)
            v.tensor_copy(rows_sb, bank[7][0:HEADS, 0:384]).then_inc(s_rows, 1)
            features(0, 0, G_F_FIRST[0])
            for k in range(KT):
                norm_lo(1, k, G_N1_HALVES[1], KT)
            features(0, 1, G_F_FIRST[1])
            split_lo(2, 0)
            v.memset(v_tok[:, 0, :], 0.0)
            ada_part(2)
            for s in range(1, 5):
                if s == 1:
                    v.wait_ge(s_zhi, 1)
                    v.tensor_tensor(z_lo[:, :, :], z_raw[:, :, :], z_hi[:, :, :], ALU.subtract).then_inc(s_zlo, 1)
                for half in range(2):
                    features(s, half, G_F + 4 * s + 2 * half)
                split_lo(s + 2, s % 2)
                if s <= 3:
                    ada_part(2 + s)
            ada_column(3, 4)
            ada_column(4, 4)
            for half in range(2):
                full(G_Z + half)
                v.tensor_copy(z_t[0:RANK, half * HALF:(half + 1) * HALF], bank[half][0:RANK, :]).then_inc(s_free, 1)
            for half in range(2):
                full(G_V + half)
                v.tensor_copy(v_tok[:, 1 + 4 * half:5 + 4 * half, :], bank[2 + half][:, :].rearrange("p (t d) -> p t d", t=4))\
                    .then_inc(s_free, 1)
            for tt in range(2):
                for half in range(2):
                    i = 2 * tt + half
                    full(G_G + i)
                    v.tensor_scalar(cum[:, tt, half * HALF:(half + 1) * HALF], bank[i][:, :], b_gate_c[:, tt:tt + 1],
                                    None, ALU.add).then_inc(s_free, 1)
            v.wait_ge(s_free, G_T)
            v.wait_ge(s_bias_full, 1)

            def gates():
                for tt in range(2):
                    y = cum[:, tt, :]
                    own.link(v.tensor_scalar(tmp_b[:, :], y, 0.0, None, ALU.min))
                    v.scalar_tensor_tensor(tmp_a[:, :], tmp_b[:, :], 2.0, y, ALU.mult, ALU.subtract).then_inc(s_gate_v, 1)
                    yield
                    v.wait_ge(s_gate_s, tt + 1)
                    own.link(v.tensor_tensor(y, tmp_b[:, :], tmp_a[:, :], ALU.subtract))
                    yield
                    for ch in range(NCH):
                        seg = cum[:, tt, ch * CHUNK:(ch + 1) * CHUNK]
                        ins = v.tensor_tensor_scan(seg, ones[:, 0:CHUNK], seg, 0.0, ALU.mult, ALU.add)
                        if ch == NCH // 2 - 1:
                            yield
                    ins.then_inc(s_gate_v, 1)
                    yield
                v.wait_ge(s_gate_v, 4)
                own.link(v.tensor_copy(cum_last3, cum[:, :, CHUNK - 1:T:CHUNK]))
                for tt in range(2):
                    yield
                    v.wait_ge(s_gate_s, 2 + 3 * tt + 2)
                    own.link(v.scalar_tensor_tensor(gq_t[:, tt, :], gq_t[:, tt, :], DK ** -0.5, tmp_a[:, :],
                                                    ALU.mult, ALU.mult))
                    c3 = cum[:, tt, :].rearrange("p (c t) -> p c t", t=CHUNK)
                    v.tensor_tensor(c3, cum_last3[:, tt, :].unsqueeze(2).broadcast_to([P, NCH, CHUNK]), c3,
                                    ALU.subtract).then_inc(s_gate_v, 1)
                    yield
                    v.wait_ge(s_gate_s, 2 + 3 * tt + 3)
                    v.tensor_tensor(gks_t[:, tt, :], gk_t[:, tt, :], tmp_a[:, :], ALU.mult).then_inc(s_gate_v, 1)
                    v.tensor_tensor(gk_t[:, tt, :], gk_t[:, tt, :], tmp_b[:, :], ALU.mult).then_inc(s_gate_v, 1)
                yield
                v.wait_ge(s_small, 64)
                own.link(v.tensor_scalar(n_sink, n_sink, -1.0, None, ALU.mult))
                v.wait_ge(s_gate_v, 10)
                v.wait_ge(s_gate_s, 8)
                for i in range(4):
                    ins = v.tensor_copy(bias[:, 2 * i:2 * i + 2, :],
                                        bank[4 + i][:, :].rearrange("p (h k) -> p h k", h=2))
                    if i % 2 == 1 and i < 3:
                        yield
                ins.then_inc(s_bias_read, 1)
                v.wait_ge(s_bias_read, 1)
                own.link(v.memset(a_mask[:, :, :], 0.0))
                v.memset(state_a[:, :, :], 0.0).then_inc(s_st_a, 1)
                yield

            gate_steps = gates()
            next(gate_steps)
            for s in range(4):
                for t in range(NT):
                    full(G_T + 8 * s + t)
                    src = bank[t % 4][:, 0:256]
                    if s < 2:
                        v.tensor_copy(gv_tok[:, t, 256 * s:256 * s + 256], src).then_inc(s_free, 1)
                    else:
                        dst = silu_g[:, t, 256 * (s - 2):256 * (s - 1)]
                        v.wait_ge(s_sg_e, 8 * (s - 2) + t + 1)
                        own.link(v.reciprocal(dst, dst))
                        v.tensor_tensor(dst, src, dst, ALU.mult).then_inc(s_free, 1)
                    next(gate_steps, None)
                if s + SLOT_T + 2 < SLOT_O:
                    split_lo(s + SLOT_T + 2, (s + SLOT_T) % 2)
                else:
                    so = SLOT_O + s - 2
                    landed(so % 2, LAND * (so // 2 + 1))
                    v.wait_ge(s_gate_copied, 1)
                    v.wait_ge(s_gn, 16)
                    gate_out_slot(so, so % 2, gate1[:, 256 * (s - 2):256 * (s - 1)])
                    split_lo(so, so % 2)
            v.wait_ge(s_free, G_O)
            v.wait_ge(s_lo, SLOT_O + 2)

            def turned(n, g):
                v.wait_ge(s_pt_full, 4 * n + 2 * g + 2)
                v.tensor_copy(prob_t[:, g, 1, :], bank[3][:, :]).then_inc(s_pt_v, 1)

            def scores(n, g, first=False):
                for j in range(2):
                    hp = 2 * g + j
                    v.wait_ge(s_sc_full, 4 * n + hp + 1)
                    if not first and j == 0:
                        v.wait_ge(s_pt_full, 4 * (n - 1) + 2 * g + 2)
                    lo = P if first else 0
                    v.scalar_tensor_tensor(prob[:, 2 * hp:2 * hp + 2, lo:256],
                                           bank[hp % 2][:, :].rearrange("p (h k) -> p h k", h=2)[:, :, lo:256],
                                           DH ** -0.5, bias[:, 2 * hp:2 * hp + 2, lo:256], ALU.mult, ALU.add)\
                        .then_inc(s_sc_free, 1)
                h = slice(4 * g, 4 * g + 4)
                v.wait_ge(s_sc_free, 4 * n + 2 * g + 2)
                own.link(v.tensor_reduce(mx[:, h], prob[:, h, :], AX.X, ALU.max))
                own.link(v.scalar_tensor_tensor(nm[:, h], mx[:, h], -1.0, n_sink[:, h], ALU.mult, ALU.min))
                v.tensor_tensor(sd[:, h], nm[:, h], n_sink[:, h], ALU.subtract).then_inc(s_nm, 1)

            def normalise(n, g):
                h = slice(4 * g, 4 * g + 4)
                v.wait_ge(s_exp, 2 * n + g + 1)
                own.link(v.tensor_tensor(den[:, h], rs[:, h], es[:, h], ALU.add))
                own.link(v.reciprocal(den[:, h], den[:, h]))
                for i in range(4 * g, 4 * g + 4):
                    ins = v.tensor_scalar(prob[:, i, :], prob[:, i, :], den[:, i:i + 1], None, ALU.mult)
                ins.then_inc(s_pn, 1)

            def mix(lo4, hi4, b, wait, count, done):
                v.wait_ge(wait, count)
                v.tensor_tensor(lo4, b[:, :].rearrange("p (t q) -> p t q", t=4), hi4, ALU.subtract).then_inc(done, 1)

            def gla_mask(n):
                for hh in range(2):
                    ins = v.copy_predicated(a_mask[:, hh:GLA_HEADS:2, :],
                                            tri[:, :].bitcast(I32).unsqueeze(1).broadcast_to([P, 2, P]),
                                            bank[(5, 7)[hh]][:, 0:2 * P].rearrange("p (h q) -> p h q", h=2))
                ins.then_inc(s_at, 1)

            def gla_state_b(n):
                v.wait_ge(s_ds_full, n + 1)
                for tt in range(2):
                    ins = v.scalar_tensor_tensor(state_b[:, tt, :], state_a[:, tt, :], dec(n, 0, tt),
                                                 bank[5][:, tt * P:(tt + 1) * P], ALU.mult, ALU.add)
                ins.then_inc(s_st_b, 1)

            def dec(n, ch, tt):
                return decay[:, ds(tt * NCH + 2 * n + ch, 1)]

            def gla_next_state(n):
                v.wait_ge(s_gsq, n + 1)
                v.tensor_scalar(gvar, gss, 1.0 / DV, EPS, ALU.mult, ALU.add).then_inc(s_gvar, 1)
                v.wait_ge(s_st_b, n + 1)
                for tt in range(2):
                    ins = v.scalar_tensor_tensor(state_a[:, tt, :], state_b[:, tt, :], dec(n, 1, tt),
                                                 bank[7][:, tt * P:(tt + 1) * P], ALU.mult, ALU.add)
                ins.then_inc(s_st_a, 1)

            def gla_finish(n):
                v.wait_ge(s_grt, n + 1)
                newton(grs, gvar, gnt)
                for h in range(GLA_HEADS):
                    sg = (silu_g[:, n, h * DV:(h + 1) * DV] if isinstance(n, int)
                          else silu_g[:, ds(n, 1), h * DV:(h + 1) * DV].squeeze(1))
                    ins = v.scalar_tensor_tensor(gla_out[:, h, :], bank[(6, 4)[h % 2]][:, h // 2 * P:(h // 2 + 1) * P], grs[:, h:h + 1], sg,
                                                 ALU.mult, ALU.mult)
                ins.then_inc(s_og, 1)

            def mix_attn(n):
                mix(act_lo[:, 0:4, ds(n * P, P)], act_hi[:, 0:4, ds(n * P, P)], bank[2], s_oa_hi, n + 1, s_oa_lo)

            def mix_gla(n):
                mix(act_lo[:, 4:8, ds(n * P, P)], act_hi[:, 4:8, ds(n * P, P)], bank[4], s_gt_hi, n + 1, s_gt_lo)

            own.link(v.memset(prob[:, :, 0:P], LOWEST))
            scores(0, 0, first=True)
            scores(0, 1, first=True)
            v.wait_ge(s_at_full, 1)
            gla_mask(0)
            normalise(0, 0)
            gla_state_b(0)
            normalise(0, 1)
            LINKS = 12
            with v.Fori(1, NT, 1) as n:
                own.enter(n - 1, LINKS)
                turned(n - 1, 0)
                scores(n, 0)
                turned(n - 1, 1)
                gla_next_state(n - 1)
                scores(n, 1)
                gla_finish(n - 1)
                normalise(n, 0)
                mix_attn(n - 1)
                v.wait_ge(s_at_full, n + 1)
                mix_gla(n - 1)
                gla_mask(n)
                gla_state_b(n)
                normalise(n, 1)
                own.leave(NT - 1)
            turned(NT - 1, 0)
            turned(NT - 1, 1)
            gla_next_state(NT - 1)
            gla_finish(NT - 1)
            mix_attn(NT - 1)
            mix_gla(NT - 1)

            for s in range(4):
                for t in range(NT):
                    full(G_O + 8 * s + t)
                    if s == 0 and t % 4 == 0:
                        v.wait_ge(s_x1[t // 4], 64)
                    d = x1[:, t, 256 * s:256 * s + 256]
                    v.tensor_tensor(d, bank[t % 4][:, 0:256], d, ALU.add).then_inc(s_free, 1)
                    if s == 3 and t == 5:
                        norm_var(0, 2)
                    if s == 3 and t == 6:
                        norm_scale(x1, x1_nrm, 0, 2)
                if s < 2:
                    so = SLOT_O + s + 2
                    landed(so % 2, LAND * (so // 2 + 1))
                    gate_out_slot(so, so % 2, gate1[:, 256 * (s + 2):256 * (s + 3)])
                    split_lo(so, so % 2)
                elif s == 2:
                    split_lo(SLOT_M, SLOT_M % 2)
            split_lo(SLOT_M + 1, (SLOT_M + 1) % 2)
            norm_var(1, 2)

            def up_lo(g, buf, stage, tiles=range(8)):
                for i in tiles:
                    slot, half, m = i // 4, (i // 2) % 2, i % 2
                    v.wait_ge(s_act, stage + i + 1)
                    cols = slice(half * HALF, (half + 1) * HALF)
                    v.tensor_tensor(hid_lo[:, buf, 2 * slot + m, cols], bank[i % 4][:, :],
                                    hid_hi[:, buf, 2 * slot + m, cols], ALU.subtract).then_inc(s_free, 1)
                    if i == 3:
                        yield 0
                yield 1

            for k in range(KT):
                norm_lo(0, k, G_N2_HALVES[0], 16)
            norm_scale(x1, x1_nrm, 1, 2)
            next(up_lo(0, 0, 24, range(0, 2)))
            for k in range(KT):
                norm_lo(1, k, G_N2_HALVES[1], 26)
            next(up_lo(0, 0, 32, range(2, 4)))

            def split_gated(s, par, half):
                landed(par, LAND * (s // 2 + 1) if isinstance(s, int) else s * (LAND // 2) + (LAND if par == 0 else LAND // 2))
                gate_slot(s, par, gate2[:, half * 512:half * 512 + 512], GROUP // P, 512)

            p0, p1 = SLOT_M % 2, (SLOT_M + 1) % 2

            def down_add(g, half, last=False):
                for t in range(NT):
                    full(g + t)
                    d = x1[:, t, half * 512:(half + 1) * 512]
                    v.tensor_tensor(d, bank[t % 4][:, :], d, ALU.add).then_inc(s_free, 1)
                    if t == 3:
                        yield 0
                yield 1

            def group_turn(g, buf, last):
                s = SLOT_M + 2 + 4 * g
                base_group = G_M + 8 + 24 * g
                ups = up_lo(g + 1, buf, 32 + 8 + 8 * g)
                next(ups)
                split_gated(s + 2, p0, 0)
                split_lo(s + 2, p0)
                next(ups)
                split_gated(s + 3, p1, 1)
                split_lo(s + 3, p1)
                adds = down_add(base_group + 8, 0)
                next(adds)
                next(adds)
                if last:
                    split_gated(s + 4, p0, 0)
                split_lo(s + 4, p0)
                adds = down_add(base_group + 16, 1)
                next(adds)
                next(adds)
                if last:
                    split_gated(s + 5, p1, 1)
                split_lo(s + 5, p1)

            split_lo(SLOT_M + 2, p0)
            next(up_lo(0, 0, 32, range(4, 8)))
            split_lo(SLOT_M + 3, p1)
            v.wait_ge(s_gate_copied, 2)
            with v.Fori(0, NG - 2, 2) as g:
                group_turn(g, 1, False)
                group_turn(g + 1, 0, False)
            group_turn(NG - 2, 1, True)

            last_group = G_M + 8 + 24 * (NG - 1)
            for _ in down_add(last_group, 0):
                pass
            v.wait_ge(s_gfin, 16)

            def final_var(t):
                v.wait_ge(s_sq, 4 + t + 1)
                v.tensor_scalar(var[:, t:t + 1], ssq[:, t:t + 1], 1.0 / D, EPS, ALU.mult, ALU.add).then_inc(s_var, 1)

            def final_scale(t):
                v.wait_ge(s_root, 4 + t + 1)
                newton(rstd[:, t:t + 1], var[:, t:t + 1], newt[:, t:t + 1])
                v.scalar_tensor_tensor(x1[:, t, :], x1[:, t, :], rstd[:, t:t + 1], gate1[:, :], ALU.mult, ALU.mult)\
                    .then_inc(s_fin, 1)

            for t in range(NT + 2):
                if t < NT:
                    full(last_group + 8 + t)
                    d = x1[:, t, 512:1024]
                    v.tensor_tensor(d, bank[t % 4][:, :], d, ALU.add).then_inc(s_free, 1)
                if t >= 2:
                    final_scale(t - 2)
                if 1 <= t <= NT:
                    final_var(t - 1)

        @block.scalar
        def _(a):
            a.preload_act_table_set("natural_log_exp_and_others")
            own = Chain(a, s_sch)

            def split_hi(s, par, used, gated=None):
                if gated is not None:
                    a.wait_ge(s_gated, gated)
                else:
                    count = (LAND * (s // 2 + 1) if isinstance(s, int)
                             else s * (LAND // 2) + (LAND if par == 0 else LAND // 2))
                    a.wait_ge(s_raw[par], count)
                if used is not None:
                    a.wait_ge(s_full, used)
                a.activation(w_hi[:, par, :], raw[:, par, :], ACT.Copy).then_inc(s_hi, 1)

            def root(y, vv, t):
                own.link(a.activation(t, vv, ACT.Ln))
                return a.activation(y, t, ACT.Exp, scale=-0.5)

            def squares(src, dst, half, ready):
                for t in range(4 * half, 4 * half + 4):
                    a.wait_ge(*ready(t))
                    ins = a.activation(dst[:, t, :], src[:, t, :], ACT.Square, accum_out=ssq[:, t:t + 1])
                ins.then_inc(s_sq, 1)

            def norm_root(half, norms):
                a.wait_ge(s_var, norms + half + 1)
                root(rstd[:, 4 * half:4 * half + 4], var[:, 4 * half:4 * half + 4], lnv[:, 4 * half:4 * half + 4])\
                    .then_inc(s_root, 1)

            def norm_hi(half, k, g, shift, scale):
                b = bank[(g + k) % 4][:, :]
                a.wait_ge(s_full, g + k + 1)
                own.link(a.activation(b, b, ACT.Identity, bias=ada_col[:, shift * KT + k:shift * KT + k + 1],
                                      scale=ada_col[:, scale * KT + k:scale * KT + k + 1]))
                a.activation(act_hi[:, k, half * HALF:(half + 1) * HALF], b, ACT.Copy).then_inc(s_act, 1)

            a.wait_ge(s_c, 16)
            a.activation(c_exp, c_in, ACT.Exp, scale=-1.0).then_inc(s_c_exp, 1)
            split_hi(0, 0, None)
            squares(x_in, x_nrm, 0, lambda t: (s_x[t], 16))
            norm_root(0, 0)
            squares(x_in, x_nrm, 1, lambda t: (s_x[t], 16))
            a.wait_ge(s_ada_col, 2)
            for k in range(KT):
                norm_hi(0, k, G_N1_HALVES[0], 0, 1)
                if k == 3:
                    norm_root(1, 0)
            split_hi(1, 1, None)
            for k in range(KT):
                norm_hi(1, k, G_N1_HALVES[1], 0, 1)
            a.wait_ge(s_z_raw, 16)
            a.activation(z_hi[:, :, :], z_raw[:, :, :], ACT.Copy).then_inc(s_zhi, 1)

            def gate_copy(row, nth):
                a.wait_ge(s_gate_full, nth)
                for h in range(2):
                    ins = a.activation(row[:, h * 512:(h + 1) * 512], bank[5 + h][:, :], ACT.Copy)
                ins.then_inc(s_gate_copied, 1)

            for s in range(2, 7):
                split_hi(s, s % 2, G_F + 4 * (s - 1))
                if s == 3:
                    gate_copy(gate1, 1)
            a.wait_ge(s_rows_out, 16)
            gate_copy(gate2, 2)
            for tt in range(2):
                a.wait_ge(s_gate_v, 2 * tt + 1)
                own.link(a.activation(tmp_a[:, :], tmp_a[:, :], ACT.Exp))
                a.activation(tmp_a[:, :], tmp_a[:, :], ACT.Ln, bias=ones[:, 0:1]).then_inc(s_gate_s, 1)
            a.wait_ge(s_gate_v, 4)
            own.link(a.activation(decay3, cum[:, :, CHUNK - 1:T:CHUNK], ACT.Exp, scale=1.0 / GATE_NORM))
            for tt in range(2):
                if tt == 1:
                    a.wait_ge(s_gate_v, 7)
                a.activation(tmp_a[:, :], cum[:, tt, :], ACT.Exp, scale=1.0 / GATE_NORM).then_inc(s_gate_s, 1)
                a.activation(tmp_b[:, :], cum[:, tt, :], ACT.Exp, scale=-1.0 / GATE_NORM).then_inc(s_gate_s, 1)
                if tt == 0:
                    split_hi(SLOT_T + 2, SLOT_T % 2, G_T + 8)
                a.wait_ge(s_gate_v, 5 + 3 * tt)
                a.activation(tmp_a[:, :], cum[:, tt, :], ACT.Exp, scale=1.0 / GATE_NORM).then_inc(s_gate_s, 1)
            for s in range(4):
                if s >= 2:
                    for t in range(NT):
                        a.wait_ge(s_full, G_T + 8 * s + t + 1)
                        dst = silu_g[:, t, 256 * (s - 2):256 * (s - 1)]
                        own.link(a.activation(dst, bank[t % 4][:, 0:256], ACT.Exp, scale=-1.0))
                        a.activation(dst, dst, ACT.Identity, bias=ones[:, 0:1]).then_inc(s_sg_e, 1)
                if s == 1:
                    split_hi(SLOT_T + 3, (SLOT_T + 1) % 2, G_T + 16)
                elif s >= 2:
                    split_hi(SLOT_O + s - 2, (SLOT_O + s) % 2, G_T + 8 * (s + 1), gated=s - 1)

            def turned(n, g):
                a.wait_ge(s_pt_full, 4 * n + 2 * g + 1)
                a.activation(prob_t[:, g, 0, :], bank[2][:, :], ACT.Copy).then_inc(s_pt_a, 1)

            def exps(n, g):
                a.wait_ge(s_nm, 2 * n + g + 1)
                for h in range(4 * g, 4 * g + 4):
                    a.activation(prob[:, h, :], prob[:, h, :], ACT.Exp, bias=nm[:, h:h + 1], accum_out=rs[:, h:h + 1])
                a.activation(es[:, 4 * g:4 * g + 4], sd[:, 4 * g:4 * g + 4], ACT.Exp).then_inc(s_exp, 1)

            def keys(n):
                a.wait_ge(s_ks_full, n + 1)
                a.activation(gks_tok[:, :], bank[6][:, 0:2 * P], ACT.Copy).then_inc(s_ks, 1)

            def mix_hi(tiles, n, b, wait, done):
                a.wait_ge(wait, n + 1)
                a.activation(act_hi[:, tiles, ds(n * P, P)], b[:, :].rearrange("p (t q) -> p t q", t=4), ACT.Copy)\
                    .then_inc(done, 1)

            def gla_squares(n):
                a.wait_ge(s_go_full, n + 1)
                for h in range(GLA_HEADS):
                    ins = a.activation(gla_out[:, h, :], bank[(6, 4)[h % 2]][:, h // 2 * P:(h // 2 + 1) * P], ACT.Square, accum_out=gss[:, h:h + 1])
                ins.then_inc(s_gsq, 1)

            def gla_root(n):
                a.wait_ge(s_gvar, n + 1)
                root(grs, gvar, gln).then_inc(s_grt, 1)

            keys(0)
            exps(0, 0)
            exps(0, 1)
            with a.Fori(1, NT, 1) as n:
                own.enter(n - 1, 1)
                turned(n - 1, 0)
                gla_squares(n - 1)
                turned(n - 1, 1)
                exps(n, 0)
                gla_root(n - 1)
                mix_hi(slice(0, 4), n - 1, bank[2], s_oa_full, s_oa_hi)
                exps(n, 1)
                mix_hi(slice(4, 8), n - 1, bank[4], s_gt_full, s_gt_hi)
                keys(n)
                own.leave(NT - 1)
            turned(NT - 1, 0)
            gla_squares(NT - 1)
            turned(NT - 1, 1)
            gla_root(NT - 1)
            mix_hi(slice(0, 4), NT - 1, bank[2], s_oa_full, s_oa_hi)
            mix_hi(slice(4, 8), NT - 1, bank[4], s_gt_full, s_gt_hi)

            split_hi(SLOT_O + 2, SLOT_O % 2, G_O + 8, gated=3)
            split_hi(SLOT_O + 3, (SLOT_O + 1) % 2, G_O + 16, gated=4)
            split_hi(SLOT_M, SLOT_M % 2, G_O + 24)

            def whole(t):
                return s_free, G_O + 24 + t + 1

            squares(x1, x1_nrm, 0, whole)
            norm_root(0, 2)
            squares(x1, x1_nrm, 1, whole)
            split_hi(SLOT_M + 1, (SLOT_M + 1) % 2, G_O + 32)
            norm_root(1, 2)

            p0, p1 = SLOT_M % 2, (SLOT_M + 1) % 2

            def up_hi(base_group, buf, tiles):
                for i in tiles:
                    slot, half, m = i // 4, (i // 2) % 2, i % 2
                    b = bank[i % 4][:, :]
                    a.wait_ge(s_full, base_group + i + 1)
                    own.link(a.activation(b, b, ACT.Relu))
                    own.link(a.activation(b, b, ACT.Square))
                    a.activation(hid_hi[:, buf, 2 * slot + m, half * HALF:(half + 1) * HALF], b, ACT.Copy)\
                        .then_inc(s_act, 1)

            def group_turn(g, buf, last):
                s = SLOT_M + 2 + 4 * g
                base_group = G_M + 8 + 24 * g
                gated = 4 + 2 * g
                up_hi(base_group, buf, range(0, 4))
                split_hi(s + 2, p0, base_group + 4, gated=gated + 1)
                up_hi(base_group, buf, range(4, 8))
                split_hi(s + 3, p1, base_group + 8, gated=gated + 2)
                split_hi(s + 4, p0, base_group + 16, gated=gated + 3 if last else None)
                split_hi(s + 5, p1, base_group + 24, gated=gated + 4 if last else None)

            for half in range(2):
                for k in range(KT):
                    norm_hi(half, k, G_N2_HALVES[half], 3, 4)
                up_hi(G_M_FIRST[half] - 2 * half, 0, range(2 * half, 2 * half + 2))
            split_hi(SLOT_M + 2, p0, G_M + 4)
            up_hi(G_M, 0, range(4, 8))
            split_hi(SLOT_M + 3, p1, G_M + 8)
            turns = (NG - 2) // 2
            with a.Fori(0, NG - 2, 2) as g:
                own.enter(0, 32)
                own.turn = g
                own.per_turn = 16
                group_turn(g, 1, False)
                group_turn(g + 1, 0, False)
                own.per_turn = 32
                own.leave(turns)
            group_turn(NG - 2, 1, True)
            for t in range(NT):
                a.wait_ge(s_free, G_M + 8 + 24 * (NG - 1) + 8 + t + 1)
                a.activation(raw[:, 0, 0:D], x1[:, t, :], ACT.Square, accum_out=ssq[:, t:t + 1]).then_inc(s_sq, 1)
                a.wait_ge(s_var, 4 + t + 1)
                root(rstd[:, t:t + 1], var[:, t:t + 1], lnv[:, t:t + 1]).then_inc(s_root, 1)


_INS = ["x", "c", "w_ada", "b_ada", "w_in", "w_gate_up", "b_gate", "gla_norm_g", "attn_sinks", "rel_bias",
        "w_out", "w_mlp_in", "w_mlp_out", "final_norm_g"]


def kernel(**inputs):
    import concourse.bacc as bacc
    from concourse.bass_utils import run_bass_kernel_spmd

    nc = bacc.Bacc("TRN2", target_bir_lowering=False, num_devices=1, dynamic_dma_scratch_size=DGE_SCRATCH)
    arrays, args = {}, []
    given = {n: np.ascontiguousarray(inputs[n]) for n in _INS}
    given.update(constants())
    for name, a in given.items():
        arrays[f"in_{name}"] = a
        args.append(nc.dram_tensor(f"in_{name}", a.shape, F32, kind="ExternalInput").ap())
    args.append(nc.dram_tensor("out", (1, T, D), F32, kind="ExternalOutput").ap())
    build(nc, *args)
    r = run_bass_kernel_spmd(nc, [arrays], core_ids=[0])
    return r.results[0]["out"]
```

```python
import numpy as np
import concourse.bass as bass
from concourse import mybir
from concourse.alu_op_type import AluOpType as ALU

F32 = mybir.dt.float32
F32R = mybir.dt.float32r
I32 = mybir.dt.int32
ACT = mybir.ActivationFunctionType
AX = mybir.AxisListType
ds = bass.ds

P = 128
D = 1024
T = 1024
KT = D // P
NT = T // P
HALF = 512
HEADS = 8
DH = 64
BUCKETS = 32
MAX_DISTANCE = 128
GLA_HEADS = 4
DK = 64
DV = 128
CHUNK = 64
RANK = 16
GATE_NORM = 16.0
EPS = 1e-6
FF = 4096
GROUP = 512
NG = FF // GROUP
NCH = T // CHUNK
Q0, K0, V0, QG0, KG0, VG0, GO0, Z0 = 0, 512, 640, 768, 1024, 1280, 1792, 2304
SLOT = 2048
LOWEST = -3.0e38
KIB = 1024
DGE_SCRATCH = 2048

SLOT_F, SLOT_T, SLOT_O, SLOT_M = 0, 5, 9, 13
G_N1 = 0
G_F = G_N1 + 16
G_N1_HALVES = (G_N1, G_N1 + 10)
G_F_FIRST = (G_N1 + 8, G_N1 + 18)
G_Z = G_F + 20
G_V = G_Z + 2
G_G = G_V + 2
G_T = G_G + 4
G_O = G_T + 16
G_N2 = G_O + 32
G_M = G_N2 + 16
G_N2_HALVES = (G_N2, G_N2 + 10)
G_M_FIRST = (G_N2 + 8, G_N2 + 18)
SLOT_LAST = SLOT_M + 4 * NG - 1
GAIN_BY_POOL = (2, 4)


def bucket_of(dist):
    max_exact = BUCKETS // 2
    d = np.maximum(dist, 0)
    large = max_exact + (np.log(np.maximum(d, max_exact) / max_exact)
                         / np.log(MAX_DISTANCE / max_exact) * (BUCKETS - max_exact)).astype(np.int32)
    return np.where(d < max_exact, d, np.minimum(large, BUCKETS - 1)).astype(np.int32)


def constants():
    onehot = np.zeros((BUCKETS + 1, 384), np.float32)
    dist = 255 - np.arange(384)
    valid = (dist >= 0) & (dist < P)
    onehot[np.where(valid, bucket_of(dist), BUCKETS), np.arange(384)] = 1.0
    j, i = np.arange(P)[:, None], np.arange(P)[None, :]
    tri = ((j <= i) & (j // CHUNK == i // CHUNK)).astype(np.float32)
    eye = np.eye(P, dtype=np.float32)
    return {"identity": eye, "reversal": eye[::-1].copy(), "bucket_onehot": onehot, "chunk_causal": tri}


class Chain:

    def __init__(self, eng, sem):
        self.eng, self.sem, self.count, self.turn, self.per_turn = eng, sem, 0, None, 0

    def link(self, instruction):
        instruction.then_inc(self.sem, 1)
        self.count += 1
        if self.turn is None:
            self.eng.wait_ge(self.sem, self.count)
        else:
            self.eng.wait_ge(self.sem, self.turn * self.per_turn + self.count)

    def enter(self, turn, per_turn):
        self.turn, self.per_turn, self.start = turn, per_turn, self.count

    def leave(self, turns):
        assert self.count - self.start == self.per_turn, (self.count, self.start, self.per_turn)
        self.count = self.start + turns * self.per_turn
        self.turn = None


def build(nc, x, c, w_ada, b_ada, w_in, w_gate_up, b_gate, gla_norm_g, attn_sinks, rel_bias,
          w_out, w_mlp_in, w_mlp_out, final_norm_g, identity, reversal, bucket_onehot, chunk_causal, out):
    x_d = x[0].rearrange("(t p) d -> p t d", p=P)
    out_d = out[0].rearrange("(t p) d -> p t d", p=P)
    w_ada_d = w_ada[0].rearrange("(p k) n -> p k n", k=KT)
    w_in_d = w_in[0].rearrange("(k p) n -> p k n", p=P)
    w_out_d = w_out[0]
    w_up_d = w_mlp_in[0].rearrange("(k p) n -> p k n", p=P)
    w_down_d = w_mlp_out[0]
    bias_rows = nc.dram_tensor("bias_rows", [HEADS, 384], F32, kind="Internal")

    base = DGE_SCRATCH + 128

    def at(kib, name, shape, dt=F32):
        return nc.alloc_sbuf_tensor_at(name, [P, *shape], dt, offset=base + int(kib * KIB))

    act_hi = at(0, "act_hi", [KT, T], F32R)
    act_lo = at(32, "act_lo", [KT, T], F32R)
    act_full = at(32, "act_full", [KT, T])
    ada_w_first = at(0, "ada_w_first", [2 * KT, D])
    x_in = at(64, "x_in", [NT, D])
    x_nrm = at(96, "x_nrm", [NT, D])
    q_t = at(64, "q_t", [4, T])
    k_t = at(80, "k_t", [P + T])
    v_tok = at(84.5, "v_tok", [NT + 1, P])
    gq_t = at(89, "gq_t", [2, T])
    gk_t = at(97, "gk_t", [2, T])
    gks_t = at(105, "gks_t", [2, T])
    gv_tok = at(113, "gv_tok", [NT, GLA_HEADS * DV])
    bias_rev = at(113, "bias_rev", [HEADS, 2 * P])
    hid_hi = at(64, "hid_hi", [2, GROUP // P, T], F32R)
    hid_lo = at(96, "hid_lo", [2, GROUP // P, T], F32R)
    x1_nrm = at(64, "x1_nrm", [NT, D])
    x1 = at(130, "x1", [NT, D])
    ada_w = at(130, "ada_w", [4, D])
    silu_g = at(130, "silu_g", [GLA_HEADS * DV])
    g_copy = at(132, "g_copy", [GLA_HEADS * DV])
    g_low = at(142, "g_low", [GLA_HEADS * DV])
    prob = at(134, "prob", [HEADS, 2 * P])
    z_t = at(130, "z_t", [T])
    w_gate = at(134, "w_gate", [GLA_HEADS * DK])
    ada_acc = at(146, "ada_acc", [2, D])
    cum = at(146, "cum", [2, T])
    bias = at(146, "bias", [HEADS, 2 * P])
    ada_b = at(154, "ada_b", [D])
    z_raw = at(158, "z_raw", [KT, RANK])
    z_hi = at(158.5, "z_hi", [KT, RANK], F32R)
    z_lo = at(159, "z_lo", [KT, RANK], F32R)
    tmp_a = at(154, "tmp_a", [T])
    tmp_b = at(158, "tmp_b", [T])
    a_mask = at(154, "a_mask", [GLA_HEADS, P])
    state_a = at(156, "state_a", [2, DV])
    state_b = at(157, "state_b", [2, DV])
    gla_out = at(158, "gla_out", [GLA_HEADS, DV])
    gks_tok = at(160, "gks_tok", [2 * P])
    raw = at(162, "raw", [2, SLOT])
    prob_t = at(162, "prob_t", [2, 2, 4 * P])
    w_hi = at(178, "w_hi", [2, SLOT], F32R)
    w_lo = at(194, "w_lo", [2, SLOT], F32R)
    gate1 = at(210, "gate1", [D])
    gate2 = at(214, "gate2", [D])
    ident = at(218, "ident", [P])
    ones = at(218.5, "ones", [P])
    tri = at(219, "tri", [P])
    small = at(220, "small", [400])
    rev = at(219.5, "rev", [P])
    taken = [0]

    def vec(n):
        taken[0] += n
        return small[:, taken[0] - n:taken[0]]

    c_in, c_exp, cond = vec(KT), vec(KT), vec(KT)
    ada_col = vec(6 * KT)
    b_gate_c = vec(2)
    b_col = vec(6 * KT)
    n_sink = vec(HEADS)
    rel_ext = vec(HEADS)
    decay, cum_last = vec(2 * NCH), vec(2 * NCH)
    ssq, var, lnv, rstd, newt = vec(NT), vec(NT), vec(NT), vec(NT), vec(NT)
    ssq_first = vec(NT)
    junk = at(162, "junk", [NT, HALF])
    mx, nm, sd, es, rs, den = (vec(HEADS) for _ in range(6))
    gss, gvar, gln, grs, gnt = (vec(GLA_HEADS) for _ in range(5))
    decay3 = decay.rearrange("p (t c) -> p t c", t=2)
    cum_last3 = cum_last.rearrange("p (t c) -> p t c", t=2)

    bank = [nc.alloc_psum_tensor(f"bank{i}", [P, 512], F32) for i in range(8)]

    def sem(name):
        return nc.alloc_semaphore(name)

    s_c, s_const, s_small = sem("c_landed"), sem("const_landed"), sem("small_landed")
    s_x = [sem(f"x_landed{i}") for i in range(NT)]
    s_ada_first = [sem(f"ada_first_landed{i}") for i in range(KT)]
    s_zeros = sem("mask_and_state_zeros")
    s_sink = sem("sinks_landed")
    s_ident = sem("identity_landed")
    s_b_rows, s_b_full, s_b_col = sem("b_rows_landed"), sem("b_col_full"), sem("b_col_ready")
    s_ada_w = [sem(f"ada_w_landed{i}") for i in range(4)]
    s_ada_b = sem("ada_b_landed")
    s_z_raw = sem("z_raw_landed")
    s_raw = [sem("raw_landed0"), sem("raw_landed1")]
    s_c_exp, s_ada_used, s_ada_sum, s_ada_full, s_gate_full, s_gate_copied, s_ada_col = (
        sem(n) for n in ("c_exp", "ada_used", "ada_summed", "ada_full", "gate_full", "gate_copied", "ada_col"))
    s_gated, s_hi, s_lo = (sem(n) for n in ("raw_gated", "slot_hi", "slot_lo"))
    s_full, s_free = sem("psum_full"), sem("psum_free")
    s_sq, s_var, s_root, s_rms = (sem(n) for n in ("squares", "variance", "root", "rms"))
    s_nrm = [sem("normed0"), sem("normed1")]
    s_set = sem("memsets")
    s_bias_full, s_bias_read = sem("bias_turned"), sem("bias_read")
    s_rows_full, s_rows, s_rows_out, s_bias = (
        sem(n) for n in ("bias_rows_full", "bias_rows_copied", "bias_rows_written", "bias_landed"))
    s_act = sem("act_stage")
    s_zhi, s_zlo = sem("z_hi_done"), sem("z_lo_done")
    s_gate_v, s_gate_s = sem("gates_by_vector"), sem("gates_by_scalar")
    s_g_copy, s_sg_sum, s_sigmoid = sem("g_out_copied"), sem("silu_summed"), sem("sigmoid_ready")
    s_sg_e, s_sg, s_sg_full = sem("silu_exp"), sem("silu_ready"), sem("g_out_full")
    s_sc_full, s_sc_free, s_nm, s_exp, s_pn = (
        sem(n) for n in ("scores_full", "scores_read", "neg_max", "exps", "probs_ready"))
    s_pt_full, s_pt_2, s_pt_3 = sem("probs_t_full"), sem("probs_t_bank2_read"), sem("probs_t_bank3_read")
    s_oa_full, s_oa_hi, s_oa_lo = sem("attn_out_full"), sem("attn_out_hi"), sem("attn_out_lo")
    s_at_full, s_at = sem("gla_a_full"), sem("gla_a_masked")
    s_ks_full, s_ks = sem("gla_ks_full"), sem("gla_ks_copied")
    s_ds_full, s_st_b, s_st_a = sem("gla_ds_full"), sem("state_b_ready"), sem("state_a_ready")
    s_go_full, s_gsq, s_gvar, s_grt, s_og = (
        sem(n) for n in ("gla_o_full", "gla_squares", "gla_variance", "gla_root", "gla_out_ready"))
    s_gt_full, s_gt_hi, s_gt_lo = sem("gla_out_t_full"), sem("gla_out_t_hi"), sem("gla_out_t_lo")
    s_x1 = [sem("x1_landed0"), sem("x1_landed1")]
    s_gfin = sem("final_gain_landed")
    s_fin, s_out = sem("final_by_vector"), sem("out_written")
    s_scaled, s_fin_pool = sem("final_scaled"), sem("final_by_gpsimd")
    s_vch, s_sch, s_pool = sem("vector_own"), sem("scalar_own"), sem("gpsimd_own")
    s_gn, s_wg = sem("gla_gain_landed"), sem("w_gate_landed")

    gate_rows = {2: gate1, 5: gate2}
    b_rows = gate1[0:6 * KT, 0:P]
    onehot_sb = gate2[0:BUCKETS + 1, 0:384]
    rows_sb = gate2[0:HEADS, 512:512 + 384]
    gain_col = vec(1)

    LAND = 64

    block = nc.Block()
    with block:
        @block.sync
        def _(sp):
            sp.dma_start(c_in, c[0].rearrange("(p k) -> p k", k=KT)).then_inc(s_c, 16)

            def ada_first(part):
                for j in range(KT // 2):
                    sp.dma_start(ada_w_first[:, part * KT + 2 * j:part * KT + 2 * j + 2, :],
                                 w_ada_d[:, 2 * j:2 * j + 2, part * D:(part + 1) * D])\
                        .then_inc(s_ada_first[part * KT // 2 + j], 16)

            def fill(s, par, sources):
                if not isinstance(s, int) or s >= 2:
                    sp.wait_ge(s_lo, s - 1)
                for dst, src in sources(par):
                    sp.dma_start(dst, src).then_inc(s_raw[par], 16)

            def raw_k(par):
                return raw[:, par, :].rearrange("p (k c) -> p k c", k=KT)

            def q_columns(s):
                return lambda par: [(raw_k(par)[:, :, m * P + g * DH:m * P + g * DH + DH],
                                     w_in_d[:, :, Q0 + g * 256 + (2 * s + m) * DH:Q0 + g * 256 + (2 * s + m) * DH + DH])
                                    for m in range(2) for g in range(2)]

            def columns(w, c0, width=256):
                return lambda par: [(raw_k(par)[:, 2 * j:2 * j + 2, :], w[:, 2 * j:2 * j + 2, ds(c0, width)])
                                    for j in range(4)]

            ada_first(0)
            sp.dma_start(b_rows, b_ada[0].rearrange("(k p) -> k p", p=P)).then_inc(s_b_rows, 16)
            sp.dma_start(ident[:, :], identity).then_inc(s_ident, 16)
            sp.dma_start(onehot_sb, bucket_onehot).then_inc(s_small, 16)
            sp.dma_start(rel_ext[0:BUCKETS, :], rel_bias).then_inc(s_small, 16)
            fill(0, 0, columns(w_in_d, QG0))
            ada_first(1)
            for t in range(NT):
                sp.dma_start(x_in[:, t, :], x_d[:, t, :]).then_inc(s_x[t], 16)
            fill(1, 1, q_columns(0))
            sp.dma_start(tri[:, :], chunk_causal).then_inc(s_const, 16)
            sp.dma_start(rev[:, :], reversal).then_inc(s_const, 16)
            sp.dma_start(n_sink, attn_sinks[0:1, :].broadcast_to([P, HEADS])).then_inc(s_sink, 16)
            with nc.allow_non_contiguous_dma(reason="256 gate biases, one a partition"):
                sp.dma_start(b_gate_c, b_gate[0].rearrange("(t p) -> p t", p=P)).then_inc(s_sink, 16)
                sp.dma_start(z_raw[:, :, :], w_in_d[:, :, Z0:Z0 + RANK]).then_inc(s_z_raw, 16)

            def out_rows(c0):
                def parts(par):
                    r = raw_k(par)
                    yield r[0:DH, 0:4, :], w_out_d[0:256, c0:c0 + 256].rearrange("(t p) n -> p t n", p=DH)
                    yield r[DH:P, 0:4, :], w_out_d[256:512, c0:c0 + 256].rearrange("(t p) n -> p t n", p=DH)
                    for j in range(2):
                        yield (r[:, 4 + 2 * j:6 + 2 * j, :],
                               w_out_d[512 + 256 * j:768 + 256 * j, c0:c0 + 256].rearrange("(t p) n -> p t n", p=P))
                return parts

            def down_rows(g, half):
                def parts(par):
                    for j in range(4):
                        yield (raw[:, par, j * 512:(j + 1) * 512],
                               w_down_d[ds(g * GROUP + j * P, P), half * 512:half * 512 + 512])
                return parts

            fill(2, 0, q_columns(1))
            for s, c0 in ((3, K0), (4, KG0)):
                fill(s, s % 2, columns(w_in_d, c0))
            sp.wait_ge(s_rows_out, 16)
            sp.wait_ge(s_free, G_F_FIRST[1])
            shifted = bass.AP(tensor=bias_rows, offset=0, ap=[[1, P], [384, HEADS], [1, 2 * P]])
            sp.dma_start(bias_rev[:, :, :], shifted).then_inc(s_bias, 16)
            for s in range(4):
                fill(SLOT_T + s, (SLOT_T + s) % 2, columns(w_in_d, VG0 + 256 * s))
            fill(SLOT_O, SLOT_O % 2, out_rows(0))
            def residual(*tiles):
                for t in tiles:
                    sp.dma_start(x1[:, t, :], x_d[:, t, :]).then_inc(s_x1[t // 4], 16)

            sp.wait_ge(s_sc_free, 4 * NT)
            residual(4, 5)
            sp.wait_ge(s_pt_full, 4 * NT)
            residual(1, 2)
            sp.wait_ge(s_og, NT)
            residual(0, 3)
            sp.wait_ge(s_oa_lo, NT)
            fill(SLOT_O + 1, (SLOT_O + 1) % 2, out_rows(256))
            sp.wait_ge(s_gt_lo, NT)
            residual(6, 7)
            fill(SLOT_O + 2, SLOT_O % 2, out_rows(512))
            fill(SLOT_O + 3, (SLOT_O + 3) % 2, out_rows(256 * 3))
            for half in range(2):
                fill(SLOT_M + half, (SLOT_M + half) % 2, columns(w_up_d, 256 * half))

            def pair(g):
                for half in range(2):
                    fill(SLOT_M + 2 + 4 * g + half, (SLOT_M + half) % 2,
                         columns(w_up_d, (g + 1) * GROUP + 256 * half))
                for half in range(2):
                    fill(SLOT_M + 4 + 4 * g + half, (SLOT_M + half) % 2, down_rows(g, half))

            with sp.Fori(0, NG - 1, 1) as g:
                pair(g)
            for half in range(2):
                fill(SLOT_LAST - 1 + half, (SLOT_M + half) % 2, down_rows(NG - 1, half))
            sp.wait_ge(s_lo, SLOT_O + 4)
            sp.dma_start(gate1[:, :], final_norm_g.rearrange("(a d) -> a d", a=1).broadcast_to([P, D]))\
                .then_inc(s_gfin, 16)
            for t in range(NT):
                if t in GAIN_BY_POOL:
                    sp.wait_ge(s_fin_pool, GAIN_BY_POOL.index(t) + 1)
                else:
                    sp.wait_ge(s_fin, t + 1 - sum(1 for i in GAIN_BY_POOL if i < t))
                sp.dma_start(out_d[:, t, :], x1[:, t, :]).then_inc(s_out, 16)
            sp.wait_ge(s_out, 16 * NT)

        @block.gpsimd
        def _(pool):
            pool.memset(ones[:, :], 1.0).then_inc(s_set, 1)
            pool.wait_ge(s_set, 1)
            pool.memset(rel_ext[BUCKETS:BUCKETS + 1, :], LOWEST).then_inc(s_set, 1)
            for part in range(2, 6):
                if part in gate_rows:
                    if part == 5:
                        pool.wait_ge(s_ada_sum, 1)
                    pool.dma_start(ada_b[0:1, :], b_ada[0:1, part * D:(part + 1) * D]).then_inc(s_ada_b, 16)
                if part == 2:
                    pool.wait_ge(s_x[NT - 1], 16)
                for k in range(KT):
                    j = (part - 2) * KT + k
                    if j >= 4:
                        pool.wait_ge(s_ada_used, 2 * KT + j - 3)
                    pool.dma_start(ada_w[:, j % 4, :], w_ada_d[:, k, part * D:(part + 1) * D])\
                        .then_inc(s_ada_w[j % 4], 16)
                if part == 2:
                    pool.wait_ge(s_rows, 1)
                    pool.dma_start(bias_rows.ap(), rows_sb).then_inc(s_rows_out, 16)
            pool.wait_ge(s_ada_used, 6 * KT)
            pool.dma_start(w_gate[0:RANK, :], w_gate_up[0]).then_inc(s_wg, 16)
            with nc.allow_non_contiguous_dma(reason="128 gains, one a partition"):
                pool.dma_start(gain_col, gla_norm_g[0].rearrange("(p a) -> p a", a=1)).then_inc(s_gn, 16)
            pool.wait_ge(s_gate_v, 10)
            pool.memset(a_mask[:, :, :], 0.0).then_inc(s_zeros, 1)
            pool.memset(state_a[:, :, :], 0.0).then_inc(s_zeros, 1)
            pool.memset(prob[:, :, 0:P], LOWEST).then_inc(s_zeros, 1)
            for n in range(NT):
                pool.wait_ge(s_g_copy, n + 1)
                pool.tensor_scalar(g_low[:, :], g_copy[:, :], -1.0, 0.0, ALU.mult, ALU.max).then_inc(s_pool, 1)
                pool.wait_ge(s_pool, n + 1)
                pool.wait_ge(s_sg_e, n + 1)
                pool.tensor_tensor(silu_g[:, :], silu_g[:, :], g_low[:, :], ALU.add).then_inc(s_sg_sum, 1)
                pool.wait_ge(s_sigmoid, n + 1)
                pool.tensor_tensor(silu_g[:, :], g_copy[:, :], silu_g[:, :], ALU.mult).then_inc(s_sg, 1)
            pool.wait_ge(s_gfin, 16)
            for i, t in enumerate(GAIN_BY_POOL):
                pool.wait_ge(s_scaled, i + 1)
                pool.tensor_tensor(x1[:, t, :], x1[:, t, :], gate1[:, :], ALU.mult).then_inc(s_fin_pool, 1)

        @block.tensor
        def _(pe):
            def act(part):
                return act_lo if part else act_hi

            def wsl(part, par):
                return (w_lo if part else w_hi)[:, par, :]

            def stationary_half(par, half, g, turned=None):
                for m in range(2):
                    if not isinstance(g, int) or g + m >= 4:
                        pe.wait_ge(s_free, g + m - 3)
                    n = 0
                    for k in range(KT):
                        if turned is not None and m == 0:
                            pe.wait_ge(s_free, turned + k)
                        for a, b in ((0, 0), (0, 1), (1, 0)):
                            w = wsl(a, par)[:, k * 256 + m * P:k * 256 + m * P + P]
                            mm = pe.matmul(bank[2 * half + m][:, :], w,
                                           act(b)[:, k, half * HALF:half * HALF + HALF],
                                           start=(n == 0), stop=(n == 3 * KT - 1))
                            n += 1
                    mm.then_inc(s_full, 1)

            def stationary_weights(s, par, g):
                pe.wait_ge(s_lo, s + 1)
                for half in range(2):
                    stationary_half(par, half, g + 2 * half)

            def moving_weights(s, par, g, tiles, stat, kt, width, split_last=False):
                pe.wait_ge(s_lo, s + 1)
                for i, t in enumerate(tiles):
                    if split_last and t == 2:
                        pe.wait_ge(s_oa_lo, NT)
                    if split_last and t == NT - 1:
                        pe.wait_ge(s_gt_lo, NT)
                    if not isinstance(g, int) or g + i >= 4:
                        pe.wait_ge(s_free, g + i - 3)
                    n = 0
                    for k in range(kt):
                        for a, b in ((0, 0), (0, 1), (1, 0)):
                            mm = pe.matmul(bank[i % 4][:, 0:width], stat(a, k, t),
                                           wsl(b, par)[:, k * width:(k + 1) * width],
                                           start=(n == 0), stop=(n == 3 * kt - 1))
                            n += 1
                    mm.then_inc(s_full, 1)

            def tok_act(a, k, t):
                return act(a)[:, k, t * P:(t + 1) * P]

            def ada(part):
                acc = ada_acc[:, part % 2, :]
                if part in gate_rows:
                    pe.wait_ge(s_ada_sum, 1 if part == 2 else 2)
                    if part == 2:
                        pe.wait_ge(s_b_col, 1)
                    if part == 5:
                        pe.wait_ge(s_gate_copied, 1)
                    for h in range(2):
                        mm = pe.matmul(bank[5 + h][:, :], ones[:, :], acc[:, h * 512:(h + 1) * 512], start=True, stop=True)
                    mm.then_inc(s_gate_full, 1)
                else:
                    pe.wait_ge(s_ada_used, (part + 1) * KT)
                    if part == 3:
                        pe.wait_ge(s_ada_col, 2)
                    for k in range(KT):
                        mm = pe.matmul(bank[4][:, part * KT + k:part * KT + k + 1], acc[:, k * P:(k + 1) * P],
                                       ones[:, 0:1], start=True, stop=True)
                    mm.then_inc(s_ada_full, 1)

            def turn_half(src, half, g, nrm):
                pe.wait_ge(s_nrm[half], nrm)
                for k in range(KT):
                    if g + k >= 4:
                        pe.wait_ge(s_free, g + k - 3)
                    for t in range(4):
                        mm = pe.transpose(bank[(g + k) % 4][:, t * P:(t + 1) * P],
                                          src[:, 4 * half + t, k * P:(k + 1) * P], ident[:, :])
                    mm.then_inc(s_full, 1)

            def turn_and_first_slot(src, norms, halves, first, s, par):
                for half in range(2):
                    turn_half(src, half, halves[half], norms)
                    if half == 0:
                        pe.wait_ge(s_lo, s + 1)
                    stationary_half(par, half, first[half], halves[half] + 1)

            pe.wait_ge(s_b_rows, 16)
            pe.wait_ge(s_ident, 16)
            pe.transpose(bank[5][:, 0:6 * KT], b_rows, ident[0:6 * KT, 0:6 * KT]).then_inc(s_b_full, 1)
            pe.wait_ge(s_set, 2)
            ada(0)
            pe.wait_ge(s_small, 32)
            pe.matmul(bank[7][0:HEADS, 0:384], rel_ext[0:BUCKETS + 1, :], onehot_sb, start=True, stop=True)\
                .then_inc(s_rows_full, 1)
            ada(1)
            turn_and_first_slot(x_nrm, 1, G_N1_HALVES, G_F_FIRST, 0, 0)
            for s in range(1, 5):
                stationary_weights(s, s % 2, G_F + 4 * s)
                ada(s + 1)
            pe.wait_ge(s_zlo, 1)
            for half in range(2):
                pe.wait_ge(s_free, G_Z + half - 3)
                n = 0
                for k in range(KT):
                    for a, b in ((0, 0), (0, 1), (1, 0)):
                        mm = pe.matmul(bank[half][0:RANK, :], (z_lo if a else z_hi)[:, k, :],
                                       act(b)[:, k, half * HALF:half * HALF + HALF],
                                       start=(n == 0), stop=(n == 3 * KT - 1))
                        n += 1
                mm.then_inc(s_full, 1)
            for half in range(2):
                pe.wait_ge(s_free, G_V + half - 3)
                for t in range(4):
                    mm = pe.transpose(bank[2 + half][:, t * P:(t + 1) * P],
                                      gks_t[:, 0, (4 * half + t) * P:(4 * half + t + 1) * P], ident[:, :])
                mm.then_inc(s_full, 1)
            pe.wait_ge(s_free, G_Z + 2)
            pe.wait_ge(s_wg, 16)
            for tt in range(2):
                for half in range(2):
                    i = 2 * tt + half
                    pe.wait_ge(s_free, G_G + i - 3)
                    pe.matmul(bank[i][:, :], w_gate[0:RANK, tt * P:(tt + 1) * P],
                              z_t[0:RANK, half * HALF:(half + 1) * HALF], start=True, stop=True).then_inc(s_full, 1)
            pe.wait_ge(s_bias, 16)
            pe.wait_ge(s_const, 32)
            pe.wait_ge(s_gate_copied, 2)
            pe.wait_ge(s_ada_col, 4)
            pe.wait_ge(s_rows, 1)
            for i in range(4):
                mm = pe.matmul(bank[4 + i][:, :], rev[:, :], bias_rev[:, 2 * i:2 * i + 2, :], start=True, stop=True)
            mm.then_inc(s_bias_full, 1)
            for s in range(2):
                moving_weights(SLOT_T + s, (SLOT_T + s) % 2, G_T + 8 * s, range(NT), tok_act, KT, 256)

            def tok(n):
                return slice(n * P, (n + 1) * P)

            def probs_turned(n, g):
                pe.wait_ge(s_pn, 2 * n + g + 1)
                for kb in range(2):
                    if g == 1:
                        pe.wait_ge((s_pt_2, s_pt_3)[kb], 2 * n + 1)
                    elif n > 0 and kb == 0:
                        pe.wait_ge(s_oa_lo, n)
                    elif kb == 1:
                        pe.wait_ge(s_sg_e, n + 1)
                    for h in range(4):
                        mm = pe.transpose(bank[2 + kb][:, h * P:(h + 1) * P],
                                          prob[:, 4 * g + h, kb * P:(kb + 1) * P], ident[:, :])
                    mm.then_inc(s_pt_full, 1)

            def attend(n):
                for g in range(2):
                    pe.wait_ge(s_pt_2, 2 * n + g + 1)
                    pe.wait_ge(s_pt_3, 2 * n + g + 1)
                for g in range(2):
                    for kb in range(2):
                        mm = pe.matmul(bank[2][g * DH:(g + 1) * DH, :], v_tok[:, n + kb, g * DH:(g + 1) * DH],
                                       prob_t[:, g, kb, :], start=(kb == 0), stop=(kb == 1))
                mm.then_inc(s_oa_full, 1)

            def out_turned(n):
                pe.wait_ge(s_og, n + 1)
                for h in range(GLA_HEADS):
                    mm = pe.transpose(bank[4][:, h * P:(h + 1) * P], gla_out[:, h, :], ident[:, :])
                mm.then_inc(s_gt_full, 1)

            def front(n, g, first=False):
                for hp in (2 * g, 2 * g + 1):
                    if not first or hp >= 2:
                        pe.wait_ge(s_sc_free, 4 * n + hp - 1)
                    for j in range(2):
                        h = 2 * hp + j
                        t = h % 4
                        q = q_t[g * DH:(g + 1) * DH, t, tok(n)]
                        if first:
                            mm = pe.matmul(bank[hp % 2][:, j * 256 + P:j * 256 + 256], q,
                                           k_t[g * DH:(g + 1) * DH, P:2 * P], start=True, stop=True)
                        else:
                            mm = pe.matmul(bank[hp % 2][:, j * 256:j * 256 + 256], q,
                                           k_t[g * DH:(g + 1) * DH, n * P:(n + 2) * P], start=True, stop=True)
                    mm.then_inc(s_sc_full, 1)

            def gla_scores(n, first=False):
                if not first:
                    pe.wait_ge(s_st_a, n)
                for h in range(GLA_HEADS):
                    r = slice((h % 2) * DK, (h % 2) * DK + DK)
                    mm = pe.matmul(bank[(5, 7)[h % 2]][:, h // 2 * P:(h // 2 + 1) * P], gk_t[r, h // 2, tok(n)],
                                   gq_t[r, h // 2, tok(n)], start=True, stop=True)
                mm.then_inc(s_at_full, 1)

            def gla_keys(n):
                if n > 0:
                    pe.wait_ge(s_og, n)
                for tt in range(2):
                    mm = pe.transpose(bank[6][:, tt * P:(tt + 1) * P], gks_t[:, tt, tok(n)], ident[:, :])
                mm.then_inc(s_ks_full, 1)

            def out_cols(h, rows):
                return bank[(6, 4)[h % 2]][rows, h // 2 * P:(h // 2 + 1) * P]

            def g_out(n, part):
                if n == 0:
                    pe.wait_ge(s_lo, SLOT_T + 3 + part)
                elif part == 0:
                    pe.wait_ge(s_pt_3, 2 * n)
                i = 0
                for k in range(KT):
                    for a, b in ((0, 0), (0, 1), (1, 0)):
                        mm = pe.matmul(bank[3][:, part * 256:part * 256 + 256], tok_act(a, k, n),
                                       wsl(b, (SLOT_T + part) % 2)[:, k * 256:(k + 1) * 256],
                                       start=(i == 0), stop=(i == 3 * KT - 1))
                        i += 1
                mm.then_inc(s_sg_full, 1)

            def gla_out_of(n):
                pe.wait_ge(s_at, n + 1)
                pe.wait_ge(s_ks, n + 1)
                for ch in range(2):
                    for h in range(GLA_HEADS):
                        r = slice(ch * CHUNK, ch * CHUNK + CHUNK)
                        gv = gv_tok[r, n, h * DV:(h + 1) * DV]
                        c0 = h // 2 * P
                        mm = pe.matmul(bank[(5, 7)[ch]][(h % 2) * DK:(h % 2) * DK + DK, c0:c0 + P],
                                       gks_tok[r, h * DK:(h + 1) * DK], gv, start=True, stop=True)
                mm.then_inc(s_ds_full, 1)
                for h in (0, 2, 1, 3):
                    if h == 1 and n > 0:
                        pe.wait_ge(s_gt_lo, n)
                    gv = gv_tok[:, n, h * DV:(h + 1) * DV]
                    pe.matmul(out_cols(h, slice(0, P)), a_mask[:, h, :], gv, start=(h < 2), stop=False,
                              skip_group_check=True)
                for ch, state in enumerate((state_a, state_b)):
                    if ch == 1:
                        pe.wait_ge(s_st_b, n + 1)
                    elif n > 0:
                        pe.wait_ge(s_st_a, n)
                    else:
                        pe.wait_ge(s_zeros, 3)
                    for h in range(GLA_HEADS):
                        r = slice((h % 2) * DK, (h % 2) * DK + DK)
                        mm = pe.matmul(out_cols(h, slice(ch * CHUNK, (ch + 1) * CHUNK)),
                                       gq_t[r, h // 2, n * P + ch * CHUNK:n * P + (ch + 1) * CHUNK], state[r, h // 2, :],
                                       start=False, stop=True, skip_group_check=True)
                mm.then_inc(s_go_full, 1)

            pe.wait_ge(s_free, G_O)
            pe.wait_ge(s_gate_v, 10)
            front(0, 0, first=True)
            g_out(0, 0)
            front(0, 1, first=True)
            pe.wait_ge(s_bias_read, 1)
            gla_scores(0, first=True)
            gla_keys(0)
            g_out(0, 1)
            gla_out_of(0)
            for n in range(1, NT):
                front(n, 0)
                probs_turned(n - 1, 0)
                probs_turned(n - 1, 1)
                front(n, 1)
                attend(n - 1)
                g_out(n, 0)
                gla_scores(n)
                out_turned(n - 1)
                gla_keys(n)
                g_out(n, 1)
                gla_out_of(n)
            for g in range(2):
                probs_turned(NT - 1, g)
            attend(NT - 1)
            out_turned(NT - 1)

            pe.wait_ge(s_pt_3, 2 * NT)
            with pe.Fori(0, 4, 2) as s:
                for j in range(2):
                    moving_weights(SLOT_O + s + j, (SLOT_O + j) % 2, G_O + 8 * (s + j), range(NT), tok_act, KT, 256,
                                   split_last=True)
            turn_and_first_slot(x1_nrm, 2, G_N2_HALVES, G_M_FIRST, SLOT_M, SLOT_M % 2)
            stationary_weights(SLOT_M + 1, (SLOT_M + 1) % 2, G_M + 4)

            def hidden(buf):
                return lambda a, k, t: (hid_lo if a else hid_hi)[:, buf, k, t * P:(t + 1) * P]

            def up(g, s, base_group):
                for half in range(2):
                    stationary_weights(s + half, (SLOT_M + half) % 2, base_group + 4 * half)

            def down(g_buf, s, base_group):
                for half in range(2):
                    moving_weights(s + half, (SLOT_M + half) % 2, base_group + 8 * half, range(NT),
                                   hidden(g_buf), GROUP // P, 512)

            def pair(g, buf):
                up(g + 1, SLOT_M + 2 + 4 * g, G_M + 8 + 24 * g)
                down(buf, SLOT_M + 4 + 4 * g, G_M + 16 + 24 * g)

            with pe.Fori(0, NG - 2, 2) as g:
                pair(g, 0)
                pair(g + 1, 1)
            pair(NG - 2, 0)
            pe.wait_ge(s_free, G_M + 8 + 24 * (NG - 2) + 8)
            down(1, SLOT_LAST - 1, G_M + 8 + 24 * (NG - 1))

        @block.vector
        def _(v):
            own = Chain(v, s_vch)

            def gate_slot(s, par, row, kt, width):
                o = raw[:, par, :].rearrange("p (k c) -> p k c", k=kt)
                v.tensor_tensor(o, o, row.unsqueeze(1).broadcast_to([P, kt, width]), ALU.mult).then_inc(s_gated, 1)

            def gate_out_slot(s, par, row):
                o = raw[:, par, :].rearrange("p (k c) -> p k c", k=KT)
                rows = row.unsqueeze(1).broadcast_to([P, KT // 2, 256])
                v.tensor_tensor(o[:, 0:KT // 2], o[:, 0:KT // 2], rows, ALU.mult)
                v.scalar_tensor_tensor(o[:, KT // 2:KT], o[:, KT // 2:KT], gain_col, rows, ALU.mult, ALU.mult)\
                    .then_inc(s_gated, 1)

            def split_lo(s, par):
                v.wait_ge(s_hi, s + 1)
                v.tensor_tensor(w_lo[:, par, :], raw[:, par, :], w_hi[:, par, :], ALU.subtract).then_inc(s_lo, 1)

            def landed(par, count):
                v.wait_ge(s_raw[par], count)

            def full(g):
                v.wait_ge(s_full, g + 1)

            def newton(y, vv, t):
                own.link(v.tensor_tensor(t, y, y, ALU.mult))
                own.link(v.tensor_tensor(t, t, vv, ALU.mult))
                own.link(v.tensor_scalar(t, t, -0.5, 1.5, ALU.mult, ALU.add))
                return v.tensor_tensor(y, y, t, ALU.mult)

            def ada_part(part):
                acc = ada_acc[:, part % 2, :]
                if part >= 2:
                    done = sum(1 for p in range(part - 1) if p not in gate_rows)
                    v.wait_ge(s_ada_full, done)
                    if part == 4:
                        v.wait_ge(s_gate_full, 1)
                for k in range(KT):
                    if part < 2:
                        v.wait_ge(s_ada_first[(part * KT + k) // 2], 16)
                        w = ada_w_first[:, part * KT + k, :]
                    else:
                        j = (part - 2) * KT + k
                        v.wait_ge(s_ada_w[j % 4], 16 * (j // 4 + 1))
                        w = ada_w[:, j % 4, :]
                    if k == 0:
                        ins = v.tensor_scalar(acc, w, cond[:, k:k + 1], None, ALU.mult)
                    else:
                        v.wait_ge(s_ada_used, part * KT + k)
                        ins = v.scalar_tensor_tensor(acc, w, cond[:, k:k + 1], acc, ALU.mult, ALU.add)
                    ins.then_inc(s_ada_used, 1)
                if part in gate_rows:
                    v.wait_ge(s_ada_used, (part + 1) * KT)
                    v.wait_ge(s_ada_b, 16 if part == 2 else 32)
                    v.tensor_tensor(acc[0:1, :], acc[0:1, :], ada_b[0:1, :], ALU.add).then_inc(s_ada_sum, 1)

            def ada_column(part, nth):
                v.wait_ge(s_ada_full, nth)
                v.scalar_tensor_tensor(ada_col[:, part * KT:(part + 1) * KT], bank[4][:, part * KT:(part + 1) * KT],
                                       1.0 if part in (1, 4) else 0.0, b_col[:, part * KT:(part + 1) * KT],
                                       ALU.add, ALU.add).then_inc(s_ada_col, 1)

            def norm_var(half, norms):
                cols = slice(4 * half, 4 * half + 4)
                v.wait_ge(s_sq, norms + half + 1)
                v.tensor_scalar(var[:, cols], ssq[:, cols], 1.0 / D, EPS, ALU.mult, ALU.add).then_inc(s_var, 1)

            def norm_newton(half, norms):
                cols = slice(4 * half, 4 * half + 4)
                v.wait_ge(s_root, norms + half + 1)
                newton(rstd[:, cols], var[:, cols], newt[:, cols]).then_inc(s_rms, 1)

            def norm_scale(src, dst, half, norms):
                norm_newton(half, norms)
                v.wait_ge(s_rms, norms + half + 1)
                for t in range(4 * half, 4 * half + 4):
                    ins = v.tensor_scalar(dst[:, t, :], src[:, t, :], rstd[:, t:t + 1], None, ALU.mult)
                ins.then_inc(s_nrm[half], 1)

            def norm_lo(half, k, g, stages, shift, scale):
                cols = slice(half * HALF, (half + 1) * HALF)
                whole = bank[(g + k) % 4][:, :]
                v.wait_ge(s_act, stages + k + 1)
                if k % 2 == 1:
                    whole = act_full[:, k, cols]
                    own.link(v.tensor_scalar(whole, bank[(g + k) % 4][:, :], ada_col[:, scale * KT + k:scale * KT + k + 1],
                                             ada_col[:, shift * KT + k:shift * KT + k + 1], ALU.mult, ALU.add))
                v.tensor_tensor(act_lo[:, k, cols], whole, act_hi[:, k, cols], ALU.subtract).then_inc(s_free, 1)

            v.wait_ge(s_c_exp, 1)
            own.link(v.tensor_scalar(c_exp, c_exp, 1.0, None, ALU.add))
            own.link(v.reciprocal(c_exp, c_exp))
            own.link(v.tensor_tensor(cond, c_in, c_exp, ALU.mult))
            ada_part(0)
            split_lo(0, 0)
            v.wait_ge(s_b_full, 1)
            v.tensor_copy(b_col, bank[5][:, 0:6 * KT]).then_inc(s_b_col, 1)
            ada_part(1)
            norm_var(0, 0)
            norm_scale(x_in, x_nrm, 0, 0)
            v.wait_ge(s_b_col, 1)
            ada_column(0, 2)
            ada_column(1, 2)
            dests = {0: [(gq_t, 0), (gq_t, 1)], 1: [(q_t, 0), (q_t, 1)], 2: [(q_t, 2), (q_t, 3)],
                     4: [(gk_t, 0), (gk_t, 1)]}

            def features(s, half, g):
                for m in range(2):
                    full(g + m)
                    if s == 3:
                        dst = (k_t[:, P + half * HALF:P + (half + 1) * HALF] if m == 0 else
                               gks_t[:, 0, half * HALF:(half + 1) * HALF])
                    else:
                        buf, tile = dests[s][m]
                        dst = buf[:, tile, half * HALF:(half + 1) * HALF]
                    v.tensor_copy(dst, bank[2 * half + m][:, :]).then_inc(s_free, 1)

            for k in range(KT):
                norm_lo(0, k, G_N1_HALVES[0], 0, 0, 1)
                if k == 2:
                    norm_var(1, 0)
            norm_scale(x_in, x_nrm, 1, 0)
            v.wait_ge(s_rows_full, 1)
            v.tensor_copy(rows_sb, bank[7][0:HEADS, 0:384]).then_inc(s_rows, 1)
            v.wait_ge(s_nrm[1], 1)
            features(0, 0, G_F_FIRST[0])
            for k in range(KT):
                norm_lo(1, k, G_N1_HALVES[1], KT, 0, 1)
            split_lo(1, 1)
            features(0, 1, G_F_FIRST[1])
            split_lo(2, 0)
            v.memset(v_tok[:, 0, :], 0.0)
            ada_part(2)
            for s in range(1, 5):
                if s == 1:
                    v.wait_ge(s_zhi, 1)
                    v.tensor_tensor(z_lo[:, :, :], z_raw[:, :, :], z_hi[:, :, :], ALU.subtract).then_inc(s_zlo, 1)
                for half in range(2):
                    features(s, half, G_F + 4 * s + 2 * half)
                split_lo(s + 2, s % 2)
                if s <= 3:
                    ada_part(2 + s)
            ada_column(3, 4)
            ada_column(4, 4)
            for half in range(2):
                full(G_Z + half)
                v.tensor_copy(z_t[0:RANK, half * HALF:(half + 1) * HALF], bank[half][0:RANK, :]).then_inc(s_free, 1)
            for half in range(2):
                full(G_V + half)
                v.tensor_copy(v_tok[:, 1 + 4 * half:5 + 4 * half, :],
                              bank[2 + half][:, :].rearrange("p (t d) -> p t d", t=4))\
                    .then_inc(s_free, 1)
            v.wait_ge(s_sink, 32)
            for tt in range(2):
                for half in range(2):
                    i = 2 * tt + half
                    full(G_G + i)
                    v.tensor_scalar(cum[:, tt, half * HALF:(half + 1) * HALF], bank[i][:, :], b_gate_c[:, tt:tt + 1],
                                    None, ALU.add).then_inc(s_free, 1)
            v.tensor_scalar(n_sink, n_sink, -1.0, None, ALU.mult)
            v.wait_ge(s_free, G_T)
            v.wait_ge(s_bias_full, 1)

            def gates():
                for tt in range(2):
                    y = cum[:, tt, :]
                    own.link(v.tensor_scalar(tmp_b[:, :], y, 0.0, None, ALU.min))
                    v.scalar_tensor_tensor(tmp_a[:, :], tmp_b[:, :], 2.0, y, ALU.mult, ALU.subtract).then_inc(s_gate_v, 1)
                    yield
                    v.wait_ge(s_gate_s, tt + 1)
                    own.link(v.tensor_tensor(y, tmp_b[:, :], tmp_a[:, :], ALU.subtract))
                    yield
                    for ch in range(NCH):
                        seg = cum[:, tt, ch * CHUNK:(ch + 1) * CHUNK]
                        ins = v.tensor_tensor_scan(seg, ones[:, 0:CHUNK], seg, 0.0, ALU.mult, ALU.add)
                        if ch == NCH // 2 - 1:
                            yield
                    ins.then_inc(s_gate_v, 1)
                    yield
                v.wait_ge(s_gate_v, 4)
                own.link(v.tensor_copy(cum_last3, cum[:, :, CHUNK - 1:T:CHUNK]))
                for tt in range(2):
                    yield
                    v.wait_ge(s_gate_s, 2 + 3 * tt + 2)
                    own.link(v.scalar_tensor_tensor(gq_t[:, tt, :], gq_t[:, tt, :], DK ** -0.5, tmp_a[:, :],
                                                    ALU.mult, ALU.mult))
                    c3 = cum[:, tt, :].rearrange("p (c t) -> p c t", t=CHUNK)
                    v.tensor_tensor(c3, cum_last3[:, tt, :].unsqueeze(2).broadcast_to([P, NCH, CHUNK]), c3,
                                    ALU.subtract).then_inc(s_gate_v, 1)
                    yield
                    v.wait_ge(s_gate_s, 2 + 3 * tt + 3)
                    v.tensor_tensor(gks_t[:, tt, :], gk_t[:, tt, :], tmp_a[:, :], ALU.mult).then_inc(s_gate_v, 1)
                    v.tensor_tensor(gk_t[:, tt, :], gk_t[:, tt, :], tmp_b[:, :], ALU.mult).then_inc(s_gate_v, 1)
            gate_steps = gates()
            next(gate_steps)
            for s in range(2):
                for t in range(NT):
                    full(G_T + 8 * s + t)
                    src = bank[t % 4][:, 0:256]
                    v.tensor_copy(gv_tok[:, t, 256 * s:256 * s + 256], src).then_inc(s_free, 1)
                    next(gate_steps, None)
                if s == 0:
                    split_lo(SLOT_T + 2, SLOT_T % 2)
            for _ in gate_steps:
                pass
            v.wait_ge(s_free, G_O)
            v.wait_ge(s_bias_read, 1)
            v.wait_ge(s_zeros, 3)

            def scores(n, g, first=False):
                for j in range(2):
                    hp = 2 * g + j
                    v.wait_ge(s_sc_full, 4 * n + hp + 1)
                    if not first and j == 0:
                        v.wait_ge(s_pt_full, 4 * (n - 1) + 2 * g + 2)
                    lo = P if first else 0
                    v.scalar_tensor_tensor(prob[:, 2 * hp:2 * hp + 2, lo:256],
                                           bank[hp % 2][:, :].rearrange("p (h k) -> p h k", h=2)[:, :, lo:256],
                                           DH ** -0.5, bias[:, 2 * hp:2 * hp + 2, lo:256], ALU.mult, ALU.add)\
                        .then_inc(s_sc_free, 1)
                h = slice(4 * g, 4 * g + 4)
                v.wait_ge(s_sc_free, 4 * n + 2 * g + 2)
                own.link(v.tensor_reduce(mx[:, h], prob[:, h, :], AX.X, ALU.max))
                own.link(v.scalar_tensor_tensor(nm[:, h], mx[:, h], -1.0, n_sink[:, h], ALU.mult, ALU.min))
                v.tensor_tensor(sd[:, h], nm[:, h], n_sink[:, h], ALU.subtract).then_inc(s_nm, 1)

            def normalise(n, g):
                h = slice(4 * g, 4 * g + 4)
                v.wait_ge(s_exp, 2 * n + g + 1)
                own.link(v.tensor_tensor(den[:, h], rs[:, h], es[:, h], ALU.add))
                own.link(v.reciprocal(den[:, h], den[:, h]))
                for i in range(4 * g, 4 * g + 4):
                    ins = v.tensor_scalar(prob[:, i, :], prob[:, i, :], den[:, i:i + 1], None, ALU.mult)
                ins.then_inc(s_pn, 1)

            def mix(lo4, hi4, b, wait, count, done):
                v.wait_ge(wait, count)
                v.tensor_tensor(lo4, b[:, :].rearrange("p (t q) -> p t q", t=4), hi4, ALU.subtract).then_inc(done, 1)

            def gla_mask(n):
                for hh in range(2):
                    ins = v.copy_predicated(a_mask[:, hh:GLA_HEADS:2, :],
                                            tri[:, :].bitcast(I32).unsqueeze(1).broadcast_to([P, 2, P]),
                                            bank[(5, 7)[hh]][:, 0:2 * P].rearrange("p (h q) -> p h q", h=2))
                ins.then_inc(s_at, 1)

            def gla_state_b(n):
                v.wait_ge(s_ds_full, n + 1)
                for tt in range(2):
                    ins = v.scalar_tensor_tensor(state_b[:, tt, :], state_a[:, tt, :], dec(n, 0, tt),
                                                 bank[5][:, tt * P:(tt + 1) * P], ALU.mult, ALU.add)
                ins.then_inc(s_st_b, 1)

            def dec(n, ch, tt):
                return decay[:, ds(tt * NCH + 2 * n + ch, 1)]

            def gla_variance(n):
                v.wait_ge(s_gsq, n + 1)
                v.tensor_scalar(gvar, gss, 1.0 / DV, EPS, ALU.mult, ALU.add).then_inc(s_gvar, 1)

            def gla_next_state(n):
                v.wait_ge(s_st_b, n + 1)
                for tt in range(2):
                    ins = v.scalar_tensor_tensor(state_a[:, tt, :], state_b[:, tt, :], dec(n, 1, tt),
                                                 bank[7][:, tt * P:(tt + 1) * P], ALU.mult, ALU.add)
                ins.then_inc(s_st_a, 1)

            def gla_finish(n):
                v.wait_ge(s_sg, n + 1)
                v.wait_ge(s_grt, n + 1)
                own.link(newton(grs, gvar, gnt))
                for h in range(GLA_HEADS):
                    ins = v.scalar_tensor_tensor(gla_out[:, h, :], bank[(6, 4)[h % 2]][:, h // 2 * P:(h // 2 + 1) * P],
                                                 grs[:, h:h + 1], silu_g[:, h * DV:(h + 1) * DV], ALU.mult, ALU.mult)
                ins.then_inc(s_og, 1)

            def mix_attn(n):
                mix(act_lo[:, 0:4, ds(n * P, P)], act_hi[:, 0:4, ds(n * P, P)], bank[2], s_oa_hi, n + 1, s_oa_lo)

            def mix_gla(n):
                mix(act_lo[:, 4:8, ds(n * P, P)], act_hi[:, 4:8, ds(n * P, P)], bank[4], s_gt_hi, n + 1, s_gt_lo)

            scores(0, 0, first=True)
            split_lo(SLOT_T + 3, (SLOT_T + 1) % 2)
            scores(0, 1, first=True)
            v.wait_ge(s_at_full, 1)
            gla_mask(0)
            normalise(0, 0)
            landed(SLOT_O % 2, LAND * (SLOT_O // 2 + 1))
            v.wait_ge(s_gate_copied, 1)
            v.wait_ge(s_gn, 16)
            gate_out_slot(SLOT_O, SLOT_O % 2, gate1[:, 0:256])
            gla_state_b(0)
            normalise(0, 1)
            LINKS = 12
            with v.Fori(1, NT, 1) as n:
                own.enter(n - 1, LINKS)
                scores(n, 0)
                gla_variance(n - 1)
                gla_next_state(n - 1)
                scores(n, 1)
                gla_finish(n - 1)
                normalise(n, 0)
                mix_attn(n - 1)
                v.wait_ge(s_at_full, n + 1)
                mix_gla(n - 1)
                gla_mask(n)
                normalise(n, 1)
                gla_state_b(n)
                own.leave(NT - 1)
            gla_variance(NT - 1)
            gla_finish(NT - 1)
            split_lo(SLOT_O, SLOT_O % 2)
            mix_attn(NT - 1)
            mix_gla(NT - 1)

            def gated_out_slot(i):
                so = SLOT_O + i
                landed(so % 2, LAND * (so // 2 + 1))
                gate_out_slot(so, so % 2, gate1[:, 256 * i:256 * (i + 1)])
                split_lo(so, so % 2)

            for s in range(4):
                for t in range(NT):
                    full(G_O + 8 * s + t)
                    if s == 0 and t % 4 == 0:
                        v.wait_ge(s_x1[t // 4], 64)
                    d = x1[:, t, 256 * s:256 * s + 256]
                    v.tensor_tensor(d, bank[t % 4][:, 0:256], d, ALU.add).then_inc(s_free, 1)
                    if s == 0 and t == 3:
                        gated_out_slot(1)
                    if s == 3 and t == 4:
                        norm_var(0, 2)
                    if s == 3 and t == 5:
                        norm_scale(x1, x1_nrm, 0, 2)
                if s < 2:
                    gated_out_slot(s + 2)
                elif s == 2:
                    split_lo(SLOT_M, SLOT_M % 2)

            def up_lo(buf, stage, tiles=range(8)):
                for i in tiles:
                    slot, half, m = i // 4, (i // 2) % 2, i % 2
                    v.wait_ge(s_act, stage + i + 1)
                    cols = slice(half * HALF, (half + 1) * HALF)
                    v.tensor_tensor(hid_lo[:, buf, 2 * slot + m, cols], bank[i % 4][:, :],
                                    hid_hi[:, buf, 2 * slot + m, cols], ALU.subtract).then_inc(s_free, 1)
                    if i == 3:
                        yield 0
                yield 1

            for k in range(KT):
                norm_lo(0, k, G_N2_HALVES[0], 16, 3, 4)
                if k == 3:
                    norm_var(1, 2)
            norm_scale(x1, x1_nrm, 1, 2)
            next(up_lo(0, 24, range(0, 2)))
            for k in range(KT):
                norm_lo(1, k, G_N2_HALVES[1], 26, 3, 4)
            split_lo(SLOT_M + 1, (SLOT_M + 1) % 2)
            next(up_lo(0, 32, range(2, 4)))

            def split_gated(s, par, half):
                landed(par, LAND * (s // 2 + 1) if isinstance(s, int) else s * (LAND // 2) + (LAND if par == 0 else LAND // 2))
                gate_slot(s, par, gate2[:, half * 512:half * 512 + 512], GROUP // P, 512)

            p0, p1 = SLOT_M % 2, (SLOT_M + 1) % 2

            def down_add(g, half):
                for t in range(NT):
                    full(g + t)
                    d = x1[:, t, half * 512:(half + 1) * 512]
                    v.tensor_tensor(d, bank[t % 4][:, :], d, ALU.add).then_inc(s_free, 1)
                    if t == 3:
                        yield 0
                yield 1

            def group_turn(g, buf, last):
                s = SLOT_M + 2 + 4 * g
                base_group = G_M + 8 + 24 * g
                ups = up_lo(buf, 32 + 8 + 8 * g)
                next(ups)
                split_gated(s + 2, p0, 0)
                split_lo(s + 2, p0)
                next(ups)
                split_gated(s + 3, p1, 1)
                split_lo(s + 3, p1)
                adds = down_add(base_group + 8, 0)
                next(adds)
                next(adds)
                if last:
                    split_gated(s + 4, p0, 0)
                split_lo(s + 4, p0)
                adds = down_add(base_group + 16, 1)
                next(adds)
                next(adds)
                if last:
                    split_gated(s + 5, p1, 1)
                split_lo(s + 5, p1)

            split_lo(SLOT_M + 2, p0)
            next(up_lo(0, 32, range(4, 8)))
            split_lo(SLOT_M + 3, p1)
            v.wait_ge(s_gate_copied, 2)
            with v.Fori(0, NG - 2, 2) as g:
                group_turn(g, 1, False)
                group_turn(g + 1, 0, False)
            group_turn(NG - 2, 1, True)

            last_group = G_M + 8 + 24 * (NG - 1)
            for _ in down_add(last_group, 0):
                pass
            v.wait_ge(s_gfin, 16)

            def final_var(t):
                v.wait_ge(s_sq, 5 + t + 1)
                v.scalar_tensor_tensor(var[:, t:t + 1], ssq[:, t:t + 1], 1.0 / D, ssq_first[:, t:t + 1],
                                       ALU.mult, ALU.add).then_inc(s_var, 1)

            def final_scale(t):
                v.wait_ge(s_root, 4 + t + 1)
                newton(rstd[:, t:t + 1], var[:, t:t + 1], newt[:, t:t + 1]).then_inc(s_rms, 1)
                if t in GAIN_BY_POOL:
                    return
                v.wait_ge(s_rms, 4 + t + 1)
                v.scalar_tensor_tensor(x1[:, t, :], x1[:, t, :], rstd[:, t:t + 1], gate1[:, :], ALU.mult, ALU.mult)\
                    .then_inc(s_fin, 1)

            for t in range(NT + 2):
                if t < NT:
                    full(last_group + 8 + t)
                    d = x1[:, t, 512:1024]
                    v.tensor_tensor(d, bank[t % 4][:, :], d, ALU.add).then_inc(s_free, 1)
                if t == 0:
                    v.wait_ge(s_sq, 5)
                    own.link(v.tensor_scalar(ssq_first, ssq_first, 1.0 / D, EPS, ALU.mult, ALU.add))
                if 1 <= t <= NT:
                    final_var(t - 1)
                if t >= 2:
                    final_scale(t - 2)

        @block.scalar
        def _(a):
            a.preload_act_table_set("natural_log_exp_and_others")
            own = Chain(a, s_sch)

            def split_hi(s, par, used, gated=None):
                if gated is not None:
                    a.wait_ge(s_gated, gated)
                else:
                    count = (LAND * (s // 2 + 1) if isinstance(s, int)
                             else s * (LAND // 2) + (LAND if par == 0 else LAND // 2))
                    a.wait_ge(s_raw[par], count)
                if used is not None:
                    a.wait_ge(s_full, used)
                a.activation(w_hi[:, par, :], raw[:, par, :], ACT.Copy).then_inc(s_hi, 1)

            def root(y, vv, t):
                own.link(a.activation(t, vv, ACT.Ln))
                return a.activation(y, t, ACT.Exp, scale=-0.5)

            def square(src, dst, t, ready):
                a.wait_ge(*ready(t))
                ins = a.activation(dst[:, t, :], src[:, t, :], ACT.Square, accum_out=ssq[:, t:t + 1])
                if t % 4 == 3:
                    ins.then_inc(s_sq, 1)

            def norm_root(half, norms):
                a.wait_ge(s_var, norms + half + 1)
                root(rstd[:, 4 * half:4 * half + 4], var[:, 4 * half:4 * half + 4], lnv[:, 4 * half:4 * half + 4])\
                    .then_inc(s_root, 1)

            def norm_hi(half, k, g, shift, scale):
                b = bank[(g + k) % 4][:, :]
                a.wait_ge(s_full, g + k + 1)
                hi = act_hi[:, k, half * HALF:(half + 1) * HALF]
                affine = dict(bias=ada_col[:, shift * KT + k:shift * KT + k + 1],
                              scale=ada_col[:, scale * KT + k:scale * KT + k + 1])
                if k % 2 == 0:
                    own.link(a.activation(b, b, ACT.Identity, **affine))
                    a.activation(hi, b, ACT.Copy).then_inc(s_act, 1)
                else:
                    a.activation(hi, b, ACT.Identity, **affine).then_inc(s_act, 1)

            a.wait_ge(s_c, 16)
            a.activation(c_exp, c_in, ACT.Exp, scale=-1.0).then_inc(s_c_exp, 1)
            split_hi(0, 0, None)
            def landed_x(t):
                return s_x[t], 16

            for t in range(4):
                square(x_in, x_nrm, t, landed_x)
            norm_root(0, 0)
            for t in range(4, NT):
                square(x_in, x_nrm, t, landed_x)
            a.wait_ge(s_ada_col, 2)
            for k in range(KT):
                norm_hi(0, k, G_N1_HALVES[0], 0, 1)
                if k == 3:
                    norm_root(1, 0)
            for k in range(KT):
                norm_hi(1, k, G_N1_HALVES[1], 0, 1)
            split_hi(1, 1, None)
            a.wait_ge(s_z_raw, 16)
            a.activation(z_hi[:, :, :], z_raw[:, :, :], ACT.Copy).then_inc(s_zhi, 1)

            def gate_copy(row, nth):
                a.wait_ge(s_gate_full, nth)
                for h in range(2):
                    ins = a.activation(row[:, h * 512:(h + 1) * 512], bank[5 + h][:, :], ACT.Copy)
                ins.then_inc(s_gate_copied, 1)

            for s in range(2, 7):
                split_hi(s, s % 2, G_F + 4 * (s - 1))
                if s == 3:
                    gate_copy(gate1, 1)
            a.wait_ge(s_rows_out, 16)
            gate_copy(gate2, 2)
            for tt in range(2):
                a.wait_ge(s_gate_v, 2 * tt + 1)
                own.link(a.activation(tmp_a[:, :], tmp_a[:, :], ACT.Exp))
                a.activation(tmp_a[:, :], tmp_a[:, :], ACT.Ln, bias=ones[:, 0:1]).then_inc(s_gate_s, 1)
            a.wait_ge(s_gate_v, 4)
            own.link(a.activation(decay3, cum[:, :, CHUNK - 1:T:CHUNK], ACT.Exp, scale=1.0 / GATE_NORM))
            for tt in range(2):
                if tt == 1:
                    a.wait_ge(s_gate_v, 7)
                a.activation(tmp_a[:, :], cum[:, tt, :], ACT.Exp, scale=1.0 / GATE_NORM).then_inc(s_gate_s, 1)
                a.activation(tmp_b[:, :], cum[:, tt, :], ACT.Exp, scale=-1.0 / GATE_NORM).then_inc(s_gate_s, 1)
                if tt == 0:
                    split_hi(SLOT_T + 2, SLOT_T % 2, G_T + 8)
                a.wait_ge(s_gate_v, 5 + 3 * tt)
                a.activation(tmp_a[:, :], cum[:, tt, :], ACT.Exp, scale=1.0 / GATE_NORM).then_inc(s_gate_s, 1)
            a.wait_ge(s_gate_v, 10)
            for i in range(4):
                ins = a.activation(bias[:, 2 * i:2 * i + 2, :], bank[4 + i][:, :].rearrange("p (h k) -> p h k", h=2),
                                   ACT.Copy)
            ins.then_inc(s_bias_read, 1)
            split_hi(SLOT_T + 3, (SLOT_T + 1) % 2, G_T + 16)

            def turned(n, g):
                a.wait_ge(s_pt_full, 4 * n + 2 * g + 1)
                a.activation(prob_t[:, g, 0, :], bank[2][:, :], ACT.Copy).then_inc(s_pt_2, 1)
                a.wait_ge(s_pt_full, 4 * n + 2 * g + 2)
                a.activation(prob_t[:, g, 1, :], bank[3][:, :], ACT.Copy).then_inc(s_pt_3, 1)

            def exps(n, g):
                a.wait_ge(s_nm, 2 * n + g + 1)
                for h in range(4 * g, 4 * g + 4):
                    a.activation(prob[:, h, :], prob[:, h, :], ACT.Exp, bias=nm[:, h:h + 1], accum_out=rs[:, h:h + 1])
                a.activation(es[:, 4 * g:4 * g + 4], sd[:, 4 * g:4 * g + 4], ACT.Exp).then_inc(s_exp, 1)

            def keys(n):
                a.wait_ge(s_ks_full, n + 1)
                a.activation(gks_tok[:, :], bank[6][:, 0:2 * P], ACT.Copy).then_inc(s_ks, 1)

            def mix_hi(tiles, n, b, wait, done):
                a.wait_ge(wait, n + 1)
                a.activation(act_hi[:, tiles, ds(n * P, P)], b[:, :].rearrange("p (t q) -> p t q", t=4), ACT.Copy)\
                    .then_inc(done, 1)

            def gla_squares(n):
                a.wait_ge(s_go_full, n + 1)
                for h in range(GLA_HEADS):
                    ins = a.activation(gla_out[:, h, :], bank[(6, 4)[h % 2]][:, h // 2 * P:(h // 2 + 1) * P],
                                       ACT.Square, accum_out=gss[:, h:h + 1])
                ins.then_inc(s_gsq, 1)

            def silu_exp(n):
                a.wait_ge(s_sg_full, 2 * n + 2)
                if not isinstance(n, int):
                    a.wait_ge(s_og, n)
                a.activation(g_copy[:, :], bank[3][:, :], ACT.Copy).then_inc(s_g_copy, 1)
                own.link(a.activation(silu_g[:, :], bank[3][:, :], ACT.Abs))
                own.link(a.activation(silu_g[:, :], silu_g[:, :], ACT.Exp, scale=-1.0))
                a.activation(silu_g[:, :], silu_g[:, :], ACT.Ln, bias=ones[:, 0:1]).then_inc(s_sg_e, 1)

            def sigmoid(n):
                a.wait_ge(s_sg_sum, n + 1)
                a.activation(silu_g[:, :], silu_g[:, :], ACT.Exp, scale=-1.0).then_inc(s_sigmoid, 1)

            def gla_root(n):
                a.wait_ge(s_gvar, n + 1)
                root(grs, gvar, gln).then_inc(s_grt, 1)

            keys(0)
            exps(0, 0)
            exps(0, 1)
            silu_exp(0)
            with a.Fori(1, NT, 1) as n:
                own.enter(n - 1, 3)
                turned(n - 1, 0)
                turned(n - 1, 1)
                gla_squares(n - 1)
                sigmoid(n - 1)
                exps(n, 0)
                gla_root(n - 1)
                mix_hi(slice(0, 4), n - 1, bank[2], s_oa_full, s_oa_hi)
                exps(n, 1)
                mix_hi(slice(4, 8), n - 1, bank[4], s_gt_full, s_gt_hi)
                keys(n)
                silu_exp(n)
                own.leave(NT - 1)
            turned(NT - 1, 0)
            gla_squares(NT - 1)
            sigmoid(NT - 1)
            gla_root(NT - 1)
            turned(NT - 1, 1)
            a.wait_ge(s_sg_full, 2 * NT)
            split_hi(SLOT_O, SLOT_O % 2, None, gated=1)
            mix_hi(slice(0, 4), NT - 1, bank[2], s_oa_full, s_oa_hi)
            mix_hi(slice(4, 8), NT - 1, bank[4], s_gt_full, s_gt_hi)

            split_hi(SLOT_O + 1, (SLOT_O + 1) % 2, None, gated=2)
            split_hi(SLOT_O + 2, SLOT_O % 2, G_O + 8, gated=3)
            split_hi(SLOT_O + 3, (SLOT_O + 1) % 2, G_O + 16, gated=4)
            split_hi(SLOT_M, SLOT_M % 2, G_O + 24)

            def whole(t):
                return s_free, G_O + 24 + t + 1

            for t in range(4):
                square(x1, x1_nrm, t, whole)
            norm_root(0, 2)
            for t in range(4, NT - 1):
                square(x1, x1_nrm, t, whole)

            p0, p1 = SLOT_M % 2, (SLOT_M + 1) % 2

            def up_hi(base_group, buf, tiles):
                for i in tiles:
                    slot, half, m = i // 4, (i // 2) % 2, i % 2
                    b = bank[i % 4][:, :]
                    a.wait_ge(s_full, base_group + i + 1)
                    own.link(a.activation(b, b, ACT.Relu))
                    own.link(a.activation(b, b, ACT.Square))
                    a.activation(hid_hi[:, buf, 2 * slot + m, half * HALF:(half + 1) * HALF], b, ACT.Copy)\
                        .then_inc(s_act, 1)

            def group_turn(g, buf, last):
                s = SLOT_M + 2 + 4 * g
                base_group = G_M + 8 + 24 * g
                gated = 4 + 2 * g
                up_hi(base_group, buf, range(0, 4))
                split_hi(s + 2, p0, base_group + 4, gated=gated + 1)
                up_hi(base_group, buf, range(4, 8))
                split_hi(s + 3, p1, base_group + 8, gated=gated + 2)
                split_hi(s + 4, p0, base_group + 16, gated=gated + 3 if last else None)
                split_hi(s + 5, p1, base_group + 24, gated=gated + 4 if last else None)

            for half in range(2):
                for k in range(KT):
                    norm_hi(half, k, G_N2_HALVES[half], 3, 4)
                    if half == 0 and k == 1:
                        square(x1, x1_nrm, NT - 1, whole)
                    if half == 0 and k == 5:
                        norm_root(1, 2)
                if half == 1:
                    split_hi(SLOT_M + 1, (SLOT_M + 1) % 2, G_O + 32)
                up_hi(G_M_FIRST[half] - 2 * half, 0, range(2 * half, 2 * half + 2))
            split_hi(SLOT_M + 2, p0, G_M + 4)
            up_hi(G_M, 0, range(4, 8))
            split_hi(SLOT_M + 3, p1, G_M + 8)
            turns = (NG - 2) // 2
            with a.Fori(0, NG - 2, 2) as g:
                own.enter(0, 32)
                own.turn = g
                own.per_turn = 16
                group_turn(g, 1, False)
                group_turn(g + 1, 0, False)
                own.per_turn = 32
                own.leave(turns)
            group_turn(NG - 2, 1, True)
            last_group = G_M + 8 + 24 * (NG - 1)
            for t in range(NT):
                a.wait_ge(s_free, last_group + t + 1)
                ins = a.activation(junk[:, t, :], x1[:, t, 0:HALF], ACT.Square, accum_out=ssq_first[:, t:t + 1])
            ins.then_inc(s_sq, 1)
            a.wait_ge(s_sq, 5)
            for t in range(NT):
                a.wait_ge(s_free, last_group + NT + t + 1)
                a.activation(junk[:, t, :], x1[:, t, HALF:D], ACT.Square, accum_out=ssq[:, t:t + 1])\
                    .then_inc(s_sq, 1)
                a.wait_ge(s_var, 4 + t + 1)
                root(rstd[:, t:t + 1], var[:, t:t + 1], lnv[:, t:t + 1]).then_inc(s_root, 1)
                if t - 1 in GAIN_BY_POOL:
                    a.wait_ge(s_rms, 4 + t)
                    a.activation(x1[:, t - 1, :], x1[:, t - 1, :], ACT.Copy, scale=rstd[:, t - 1:t])\
                        .then_inc(s_scaled, 1)


_INS = ["x", "c", "w_ada", "b_ada", "w_in", "w_gate_up", "b_gate", "gla_norm_g", "attn_sinks", "rel_bias",
        "w_out", "w_mlp_in", "w_mlp_out", "final_norm_g"]


def kernel(**inputs):
    import concourse.bacc as bacc
    from concourse.bass_utils import run_bass_kernel_spmd

    nc = bacc.Bacc("TRN2", target_bir_lowering=False, num_devices=1, dynamic_dma_scratch_size=DGE_SCRATCH)
    arrays, args = {}, []
    given = {n: np.ascontiguousarray(inputs[n]) for n in _INS}
    given.update(constants())
    for name, a in given.items():
        arrays[f"in_{name}"] = a
        args.append(nc.dram_tensor(f"in_{name}", a.shape, F32, kind="ExternalInput").ap())
    args.append(nc.dram_tensor("out", (1, T, D), F32, kind="ExternalOutput").ap())
    build(nc, *args)
    r = run_bass_kernel_spmd(nc, [arrays], core_ids=[0])
    return r.results[0]["out"]
```
